# Optimizing a Trainium2 kernel written in Bass

```python
import jax, jax.numpy as jnp
from jax import lax
import numpy as np

D_MODEL = 1024
BATCH = 1
SEQ = 2048
DEPTH = 1
DEC_BATCH = 1
DEC_SEQ = 512
PAST_LEN = 128

N_MIXERS = 4
D_FF = 4 * D_MODEL
EPS = 1e-6
POOL_WINDOWS = (2, 4, 8, 16)
N_POOL_GROUPS = len(POOL_WINDOWS)
POOL_GROUP = D_MODEL // N_POOL_GROUPS
CONV_WIDTH = 31
SGU_WIDTH = D_MODEL
SGU_HEADS = 4
SGU_HEAD_DIM = SGU_WIDTH // SGU_HEADS
SGU_CHUNK = 128
FNET_GROUPS = 4
FNET_GROUP = D_MODEL // FNET_GROUPS
N_POOL_LAYERS = (DEPTH - 0 + N_MIXERS - 1) // N_MIXERS
N_CONV_LAYERS = (DEPTH - 1 + N_MIXERS - 1) // N_MIXERS
N_SGU_LAYERS = (DEPTH - 2 + N_MIXERS - 1) // N_MIXERS
N_FNET_LAYERS = (DEPTH - 3 + N_MIXERS - 1) // N_MIXERS

kernel_name = "interleaved_pool_conv_sgu_fourier_encoder"

def rms_norm(x, g):
    xf = x.astype(jnp.float32)
    y = xf * lax.rsqrt(jnp.mean(xf * xf, axis=-1, keepdims=True) + EPS)
    return (y * g.astype(jnp.float32)).astype(x.dtype)

def layer_norm(x, g, b):
    xf = x.astype(jnp.float32)
    mu = jnp.mean(xf, axis=-1, keepdims=True)
    xc = xf - mu
    var = jnp.mean(xc * xc, axis=-1, keepdims=True)
    y = xc * lax.rsqrt(var + EPS) * g.astype(jnp.float32) + b.astype(jnp.float32)
    return y.astype(x.dtype)

def pool_mixer(h, w, scale):
    B, S, D = h.shape
    hf = h.astype(jnp.float32)
    cs = jnp.concatenate([jnp.zeros((B, 1, D), jnp.float32), jnp.cumsum(hf, axis=1)], axis=1)
    t = jnp.arange(S)
    outs = []
    for g, win in enumerate(POOL_WINDOWS):
        lo = jnp.maximum(t - win // 2, 0)
        hi = jnp.minimum(t + win // 2, S)
        sl = slice(g * POOL_GROUP, (g + 1) * POOL_GROUP)
        csg = cs[:, :, sl]
        cnt = (hi - lo).astype(jnp.float32)[None, :, None]
        mean = (jnp.take(csg, hi, axis=1) - jnp.take(csg, lo, axis=1)) / cnt
        outs.append(mean - hf[:, :, sl])
    d = jnp.stack(outs, axis=2).astype(h.dtype)
    y = jnp.einsum('bsgc,gce->bsge', d, w).reshape(B, S, D)
    return y * scale

def conv_mixer(h, w_in, b_in, dw, dw_b, ln_g, ln_b, w_out, b_out):
    a = jnp.einsum('bsd,de->bse', h, w_in) + b_in
    val, gate = jnp.split(a, 2, axis=-1)
    g = val * jax.nn.sigmoid(gate)
    pad = CONV_WIDTH // 2
    c = lax.conv_general_dilated(
        g, dw[:, None, :], window_strides=(1,), padding=[(pad, pad)],
        dimension_numbers=('NWC', 'WIO', 'NWC'), feature_group_count=D_MODEL) + dw_b
    c = jax.nn.silu(layer_norm(c, ln_g, ln_b))
    return jnp.einsum('bsd,de->bse', c, w_out) + b_out

def sgu_mixer(h, w_in, b_in, ln_g, ln_b, ws, bs, w_out, b_out):
    B, S, _ = h.shape
    z = jax.nn.gelu(jnp.einsum('bsd,de->bse', h, w_in) + b_in)
    u, v = jnp.split(z, 2, axis=-1)
    v = layer_norm(v, ln_g, ln_b)
    v = v.reshape(B, S // SGU_CHUNK, SGU_CHUNK, SGU_HEADS, SGU_HEAD_DIM)
    v = jnp.einsum('hqp,bcphd->bcqhd', ws, v) + bs.T[:, :, None]
    y = u * v.reshape(B, S, SGU_WIDTH)
    return jnp.einsum('bse,ed->bsd', y, w_out) + b_out

def fourier_mixer(h, w_out, b_out):
    B, S, D = h.shape
    hg = h.astype(jnp.float32).reshape(B, S, FNET_GROUPS, FNET_GROUP)
    f = jnp.fft.fftn(hg, axes=(1, 3), norm='ortho').real.astype(h.dtype).reshape(B, S, D)
    return jnp.einsum('bsd,de->bse', f, w_out) + b_out

def sqrelu_mlp(h, w_up, w_down):
    a = jax.nn.relu(jnp.einsum('bsd,df->bsf', h, w_up))
    return jnp.einsum('bsf,fd->bsd', a * a, w_down)

def trunk(x, norm_mix_g, norm_mlp_g, w_up, w_down, final_norm_g,
          pool_w, pool_scale,
          conv_w_in, conv_b_in, conv_dw, conv_dw_b, conv_ln_g, conv_ln_b, conv_w_out, conv_b_out,
          sgu_w_in, sgu_b_in, sgu_ln_g, sgu_ln_b, sgu_ws, sgu_bs, sgu_w_out, sgu_b_out,
          fnet_w_out, fnet_b_out):
    for i in range(DEPTH):
        m, j = i % N_MIXERS, i // N_MIXERS
        h = rms_norm(x, norm_mix_g[i])
        if m == 0:
            y = pool_mixer(h, pool_w[j], pool_scale[j])
        elif m == 1:
            y = conv_mixer(h, conv_w_in[j], conv_b_in[j], conv_dw[j], conv_dw_b[j],
                           conv_ln_g[j], conv_ln_b[j], conv_w_out[j], conv_b_out[j])
        elif m == 2:
            y = sgu_mixer(h, sgu_w_in[j], sgu_b_in[j], sgu_ln_g[j], sgu_ln_b[j],
                          sgu_ws[j], sgu_bs[j], sgu_w_out[j], sgu_b_out[j])
        else:
            y = fourier_mixer(h, fnet_w_out[j], fnet_b_out[j])
        x = x + y
        x = x + sqrelu_mlp(rms_norm(x, norm_mlp_g[i]), w_up[i], w_down[i])
    return rms_norm(x, final_norm_g)

def setup_inputs(seed: int = 0) -> dict:
    key = jax.random.key(seed)
    ks = jax.random.split(key, 32)
    D = D_MODEL

    def nrm(k, shape, scale):
        return jax.random.normal(k, shape, jnp.float32) * scale

    def gain(k, shape):
        return 1.0 + 0.05 * jax.random.normal(k, shape, jnp.float32)

    return {
        "x_prompt": nrm(ks[0], (BATCH, SEQ, D), 1.0),
        "x_sample": nrm(ks[1], (DEC_BATCH, DEC_SEQ, D), 1.0),
        "norm_mix_g": gain(ks[2], (DEPTH, D)),
        "norm_mlp_g": gain(ks[3], (DEPTH, D)),
        "w_up": nrm(ks[4], (DEPTH, D, D_FF), D ** -0.5),
        "w_down": nrm(ks[5], (DEPTH, D_FF, D), D_FF ** -0.5),
        "final_norm_g": gain(ks[6], (D,)),
        "pool_w": nrm(ks[7], (N_POOL_LAYERS, N_POOL_GROUPS, POOL_GROUP, POOL_GROUP), POOL_GROUP ** -0.5),
        "pool_scale": gain(ks[8], (N_POOL_LAYERS, D)),
        "conv_w_in": nrm(ks[9], (N_CONV_LAYERS, D, 2 * D), D ** -0.5),
        "conv_b_in": nrm(ks[10], (N_CONV_LAYERS, 2 * D), 0.02),
        "conv_dw": nrm(ks[11], (N_CONV_LAYERS, CONV_WIDTH, D), CONV_WIDTH ** -0.5),
        "conv_dw_b": nrm(ks[12], (N_CONV_LAYERS, D), 0.02),
        "conv_ln_g": gain(ks[13], (N_CONV_LAYERS, D)),
        "conv_ln_b": nrm(ks[14], (N_CONV_LAYERS, D), 0.02),
        "conv_w_out": nrm(ks[15], (N_CONV_LAYERS, D, D), D ** -0.5),
        "conv_b_out": nrm(ks[16], (N_CONV_LAYERS, D), 0.02),
        "sgu_w_in": nrm(ks[17], (N_SGU_LAYERS, D, 2 * SGU_WIDTH), D ** -0.5),
        "sgu_b_in": nrm(ks[18], (N_SGU_LAYERS, 2 * SGU_WIDTH), 0.02),
        "sgu_ln_g": gain(ks[19], (N_SGU_LAYERS, SGU_WIDTH)),
        "sgu_ln_b": nrm(ks[20], (N_SGU_LAYERS, SGU_WIDTH), 0.02),
        "sgu_ws": nrm(ks[21], (N_SGU_LAYERS, SGU_HEADS, SGU_CHUNK, SGU_CHUNK), SGU_CHUNK ** -0.5),
        "sgu_bs": gain(ks[22], (N_SGU_LAYERS, SGU_HEADS, SGU_CHUNK)),
        "sgu_w_out": nrm(ks[23], (N_SGU_LAYERS, SGU_WIDTH, D), SGU_WIDTH ** -0.5),
        "sgu_b_out": nrm(ks[24], (N_SGU_LAYERS, D), 0.02),
        "fnet_w_out": nrm(ks[25], (N_FNET_LAYERS, D, D), D ** -0.5),
        "fnet_b_out": nrm(ks[26], (N_FNET_LAYERS, D), 0.02),
    }

def reference(x_prompt, x_sample, norm_mix_g, norm_mlp_g, w_up, w_down, final_norm_g,
              pool_w, pool_scale,
              conv_w_in, conv_b_in, conv_dw, conv_dw_b, conv_ln_g, conv_ln_b, conv_w_out, conv_b_out,
              sgu_w_in, sgu_b_in, sgu_ln_g, sgu_ln_b, sgu_ws, sgu_bs, sgu_w_out, sgu_b_out,
              fnet_w_out, fnet_b_out):
    params = (norm_mix_g, norm_mlp_g, w_up, w_down, final_norm_g,
              pool_w, pool_scale,
              conv_w_in, conv_b_in, conv_dw, conv_dw_b, conv_ln_g, conv_ln_b, conv_w_out, conv_b_out,
              sgu_w_in, sgu_b_in, sgu_ln_g, sgu_ln_b, sgu_ws, sgu_bs, sgu_w_out, sgu_b_out,
              fnet_w_out, fnet_b_out)
    y_prompt = trunk(x_prompt, *params)
    y_sample = trunk(x_sample, *params)
    return (y_prompt, y_sample)


_drawn_inputs = setup_inputs


def setup_inputs(seed=0):
    import zlib

    import numpy as np

    out = dict(_drawn_inputs(seed))
    spreads = {}
    factors = {}
    for name, (base, spread) in spreads.items():
        noise = np.random.default_rng([zlib.crc32(name.encode()), seed]).standard_normal(out[name].shape)
        drawn = base * np.exp(spread * noise) if base else spread * noise
        out[name] = __import__('jax').numpy.asarray(drawn.astype(out[name].dtype))
    for name, factor in factors.items():
        out[name] = (out[name] * factor).astype(out[name].dtype)
    return out
```

```python
from contextlib import ExitStack

import concourse.bass as bass
from concourse import mybir
from concourse.alu_op_type import AluOpType as ALU

P = 128
D = 1024
F = 4096
GT = 512
GROUPS = 5
EPS = 1e-6
WINDOWS = 4
WC = D // WINDOWS
CT = WC // P
HALO = 8
PIECE = P - 2 * HALO
PIECES = -(-GT // PIECE)
LAST = GT - (PIECES - 1) * PIECE
LAST_ROWS = LAST + 2 * HALO
XROWS = GT + 2 * HALO
FC = 256
CHUNKS = F // FC
FT = FC // P
DT = D // P
TT = GT // P
HALF = 512
NH = D // HALF
OUTS = TT * NH
RING = 4
MIX_PAIRS = WINDOWS
PAIRS = CHUNKS // 2
PAIR_OUTS = 2 * OUTS
MIX_PAIR_OUTS = PAIR_OUTS + TT
GROUP_OUTS = PAIRS * PAIR_OUTS + WINDOWS * TT
FIRST_OUTS = WINDOWS * TT


def build(nc, xg, w_up, w_down, pool_w, pool_scale, g_mix, g_mlp, g_fin,
          band_first, band_mid, band_last, ident_in, out):
    f32 = mybir.dt.float32
    f32r = mybir.dt.float32r
    ACT = mybir.ActivationFunctionType
    ds = bass.ds

    w_up_v = w_up.rearrange("(t p) f -> p t f", p=P)
    w_down_v = w_down.rearrange("(t p) d -> p t d", p=P)
    pool_w_v = pool_w.rearrange("g (t p) e -> p (g t) e", p=P)

    ctx = ExitStack()
    with ctx:
        def sb(name, shape, dt=f32):
            return ctx.enter_context(nc.sbuf_tensor(name, shape, dt))

        def pb(name, shape):
            return ctx.enter_context(nc.psum_tensor(name, shape, f32))

        def sem(name):
            return ctx.enter_context(nc.semaphore(name))

        h2_hi = sb("h2_hi", [P, DT, GT], f32r)
        h2_lo = sb("h2_lo", [P, DT, GT], f32r)
        wu_raw = sb("wu_raw", [P, DT, FC])
        wu_hi = sb("wu_hi", [P, DT, FC], f32r)
        wu_lo = sb("wu_lo", [P, DT, FC], f32r)
        wd_raw = sb("wd_raw", [P, FT, D])
        wd_hi = sb("wd_hi", [P, FT, D], f32r)
        wd_lo = sb("wd_lo", [P, FT, D], f32r)
        relu = sb("relu", [P, FT, GT])
        square = sb("square", [P, FT, GT])
        a_hi = sb("a_hi", [P, 2, FT, GT], f32r)
        a_lo = sb("a_lo", [P, 2, FT, GT], f32r)
        acc = sb("acc", [P, TT, D])
        xp = sb("xp", [P, PIECES, D])
        xw_hi = sb("xw_hi", [P, PIECES * WC], f32r)
        xw_lo = sb("xw_lo", [P, PIECES * WC], f32r)
        dt_hi = sb("dt_hi", [P, CT, GT], f32r)
        dt_lo = sb("dt_lo", [P, CT, GT], f32r)
        x1 = sb("x1", [P, TT, D])
        pw_hi = sb("pw_hi", [P, WINDOWS * CT, WC], f32r)
        pw_lo = sb("pw_lo", [P, WINDOWS * CT, WC], f32r)
        bm_hi = sb("bm_hi", [P, WINDOWS, PIECE], f32r)
        bf_hi = sb("bf_hi", [P, WINDOWS, PIECE], f32r)
        bf_lo = sb("bf_lo", [P, WINDOWS, PIECE], f32r)
        bl_hi = sb("bl_hi", [P, WINDOWS, LAST], f32r)
        bl_lo = sb("bl_lo", [P, WINDOWS, LAST], f32r)
        bf_raw = sb("bf_raw", [P, WINDOWS, PIECE])
        bl_raw = sb("bl_raw", [P, WINDOWS, LAST])
        g_fin_b = sb("g_fin_b", [P, D])
        g_mix_c = sb("g_mix_c", [P, DT])
        g_mlp_c = sb("g_mlp_c", [P, DT])
        ident = sb("ident", [P, P])
        power = sb("power", [P, PIECES])
        eps = sb("eps", [P, PIECES])
        ms_x = sb("ms_x", [P, PIECES])
        me_x = sb("me_x", [P, PIECES])
        rs_x = sb("rs_x", [P, PIECES])
        ms_m = sb("ms_m", [P, TT])
        me_m = sb("me_m", [P, TT])
        rs_m = sb("rs_m", [P, TT])
        ms_f = sb("ms_f", [P, TT])
        me_f = sb("me_f", [P, TT])
        rs_f = sb("rs_f", [P, TT])
        pw_raw = acc[:, 0:2, :].rearrange("p a (b e) -> p (a b) e", e=WC)
        scale_b = acc[:, 2, :]
        bm_raw = bf_raw

        up_ps = pb("up_ps", [P, FT, HALF])
        ring_ps = pb("ring_ps", [P, RING, HALF])
        mix_ps = pb("mix_ps", [P, 2, HALF])

        const_in = sem("const_in")
        band_mid_in = sem("band_mid_in")
        const_set = sem("const_set")
        pool_scaled = sem("pool_scaled")
        pool_hi = sem("pool_hi")
        pool_lo = sem("pool_lo")
        band_mid_hi = sem("band_mid_hi")
        wu_in = sem("wu_in")
        wu_hi_done = sem("wu_hi_done")
        wu_lo_done = sem("wu_lo_done")
        wd_in = sem("wd_in")
        wd_hi_done = sem("wd_hi_done")
        wd_lo_done = sem("wd_lo_done")
        up_done = sem("up_done")
        relu_done = sem("relu_done")
        square_done = sem("square_done")
        a_hi_done = sem("a_hi_done")
        a_lo_done = sem("a_lo_done")
        ring_full = sem("ring_full")
        ring_read = sem("ring_read")
        xp_in = sem("xp_in")
        band_in = sem("band_in")
        x1_in = sem("x1_in")
        band_hi_done = sem("band_hi_done")
        band_lo_done = sem("band_lo_done")
        ms_x_done = sem("ms_x_done")
        me_x_done = sem("me_x_done")
        rs_x_done = sem("rs_x_done")
        xw_hi_done = sem("xw_hi_done")
        xw_lo_done = sem("xw_lo_done")
        pooled = sem("pooled")
        dt_hi_done = sem("dt_hi_done")
        dt_lo_done = sem("dt_lo_done")
        ms_m_done = sem("ms_m_done")
        me_m_done = sem("me_m_done")
        rs_m_done = sem("rs_m_done")
        x1n_done = sem("x1n_done")
        transposed = sem("transposed")
        h2_hi_done = sem("h2_hi_done")
        h2_lo_done = sem("h2_lo_done")
        acc_set = sem("acc_set")
        ms_f_done = sem("ms_f_done")
        me_f_done = sem("me_f_done")
        rs_f_done = sem("rs_f_done")
        final_done = sem("final_done")
        stored = sem("stored")

        block = ctx.enter_context(nc.Block())

        def ring_base(g):
            return FIRST_OUTS + g * GROUP_OUTS

        LAST_BASE = ring_base(GROUPS - 1)
        MIX_END = MIX_PAIRS * MIX_PAIR_OUTS

        @block.sync
        def _(sp):
            def load_wu(n, k):
                sp.dma_start(wu_raw[:, :, :], w_up_v[:, :, ds(k * FC, FC)]).then_inc(wu_in, 16)

            def load_wd(n, k):
                sp.dma_start(wd_raw[:, :, :], w_down_v[:, ds(k * FT, FT), :]).then_inc(wd_in, 16)

            def step(n, k, k_next):
                sp.wait_ge(wu_lo_done, 2 * n + 2)
                load_wu(n + 1, k_next)
                sp.wait_ge(wd_lo_done, 2 * n)
                load_wd(n, k)

            def load_pieces(m):
                for p in range(PIECES):
                    rows = P if p < PIECES - 1 else LAST_ROWS
                    sp.dma_start(xp[0:rows, p, :], xg[m, p * PIECE:p * PIECE + rows, :]).then_inc(xp_in, 16)

            def load_bands(m):
                sp.dma_start(bf_raw[:, :, :], band_first[m]).then_inc(band_in, 16)
                sp.dma_start(bl_raw[0:LAST_ROWS, :, :], band_last[m]).then_inc(band_in, 16)

            load_pieces(0)
            sp.dma_start(bm_raw[:, :, :], band_mid).then_inc(band_mid_in, 16)
            sp.dma_start(pw_raw, pool_w_v).then_inc(const_in, 16)
            sp.dma_start(scale_b, pool_scale.partition_broadcast(P)).then_inc(const_in, 16)
            sp.dma_start(g_mix_c[:, :], g_mix).then_inc(const_in, 16)
            sp.dma_start(g_mlp_c[:, :], g_mlp).then_inc(const_in, 16)
            sp.dma_start(g_fin_b[:, :], g_fin.partition_broadcast(P)).then_inc(const_in, 16)
            sp.dma_start(ident[:, :], ident_in).then_inc(const_in, 16)
            load_wu(0, 0)
            load_wd(0, 0)
            sp.wait_ge(band_mid_hi, 1)
            load_bands(0)
            sp.wait_ge(wu_lo_done, 2)
            load_wu(1, 1)

            def group_steps(g):
                n0 = CHUNKS * g
                with sp.Fori(0, PAIRS - 1) as i:
                    for s in (1, 2):
                        step(n0 + 2 * i + s, 2 * i + s, 2 * i + s + 1)

            with sp.Fori(0, GROUPS - 1) as g:
                sp.wait_ge(transposed, DT * (g + 1))
                load_pieces(g + 1)
                sp.wait_ge(band_lo_done, 2 * (g + 1))
                load_bands(g + 1)
                group_steps(g)
                n0 = CHUNKS * g
                step(n0 + CHUNKS - 1, CHUNKS - 1, 0)
                step(n0 + CHUNKS, 0, 1)
            n0 = CHUNKS * (GROUPS - 1)
            group_steps(GROUPS - 1)
            sp.wait_ge(wd_lo_done, 2 * (n0 + CHUNKS - 1))
            load_wd(n0 + CHUNKS - 1, CHUNKS - 1)

        @block.scalar
        def _(act):
            def split_wu(n):
                for h in range(2):
                    act.wait_ge(wu_in, 16 * (n + 1))
                    act.wait_ge(up_done, FT * n)
                    s = slice(h * DT // 2, (h + 1) * DT // 2)
                    nc.scalar.copy(wu_hi[:, s, :], wu_raw[:, s, :]).then_inc(wu_hi_done, 1)

            def split_wd(n, outs_before):
                for t in range(FT):
                    act.wait_ge(wd_in, 16 * (n + 1))
                    act.wait_ge(ring_full, outs_before)
                    nc.scalar.copy(wd_hi[:, t, :], wd_raw[:, t, :]).then_inc(wd_hi_done, 1)

            def activate(n, slot, first=False):
                for t in range(FT):
                    act.wait_ge(up_done, FT * n + t + 1)
                    if not first:
                        act.wait_ge(square_done, FT * (n - 1) + t + 1)
                    nc.scalar.activation(relu[:, t, :], up_ps[:, t, :], ACT.Relu).then_inc(relu_done, 1)
                    act.wait_ge(relu_done, FT * n + t + 1)
                    nc.scalar.activation(a_hi[:, slot, t, :], relu[:, t, :], ACT.Square).then_inc(a_hi_done, 1)

            def mean_square(junk, src, dst):
                return nc.scalar.activation(junk, src, ACT.Square, scale=D ** -0.5, accum_out=dst)

            def piece_stats(m):
                for p in range(PIECES):
                    rows = P if p < PIECES - 1 else LAST_ROWS
                    act.wait_ge(xp_in, 16 * (PIECES * m + PIECES))
                    if p > 0:
                        act.wait_ge(ms_x_done, PIECES * m + p)
                    mean_square(xw_hi[0:rows, 0:D], xp[0:rows, p, :], ms_x[0:rows, p:p + 1]).then_inc(ms_x_done, 1)

            def split_bands(m):
                act.wait_ge(band_in, 32 * (m + 1))
                nc.scalar.copy(bf_hi[:, :, :], bf_raw[:, :, :]).then_inc(band_hi_done, 1)
                nc.scalar.copy(bl_hi[0:LAST_ROWS, :, :], bl_raw[0:LAST_ROWS, :, :]).then_inc(band_hi_done, 1)

            def split_pieces(m, w, first=False):
                act.wait_ge(rs_x_done, m + 1)
                if not first:
                    act.wait_ge(pooled, CT * (WINDOWS * m + w))
                for p in range(PIECES):
                    rows = P if p < PIECES - 1 else LAST_ROWS
                    nc.scalar.activation(xw_hi[0:rows, p * WC:(p + 1) * WC], xp[0:rows, p, ds(w * WC, WC)],
                                         ACT.Copy, scale=rs_x[0:rows, p:p + 1]).then_inc(xw_hi_done, 1)

            def split_pooled(m, w):
                for c in range(CT):
                    act.wait_ge(pooled, CT * (WINDOWS * m + w) + c + 1)
                    nc.scalar.copy(dt_hi[:, c, :], mix_ps[:, c, :]).then_inc(dt_hi_done, 1)

            def mixed_stats(m, outs):
                act.wait_ge(ring_read, outs)
                for j in range(TT):
                    if j > 0:
                        act.wait_ge(ms_m_done, TT * m + j)
                    mean_square(xw_hi[:, 0:D], x1[:, j, :], ms_m[:, j:j + 1]).then_inc(ms_m_done, 1)

            def norm_mixed(m):
                act.wait_ge(rs_m_done, m + 1)
                act.wait_ge(xw_lo_done, PIECES * WINDOWS * (m + 1))
                for j in range(TT):
                    nc.scalar.activation(xp[:, j, :], x1[:, j, :], ACT.Copy,
                                         scale=rs_m[:, j:j + 1]).then_inc(x1n_done, 1)

            def split_h2(m, d):
                act.wait_ge(transposed, DT * m + d + 1)
                nc.scalar.activation(h2_hi[:, d, :], mix_ps[:, d % 2, :], ACT.Copy,
                                     scale=g_mlp_c[:, d:d + 1]).then_inc(h2_hi_done, 1)

            def final_stats(g, outs_before):
                for j in range(TT):
                    act.wait_ge(ring_read, outs_before + NH * (j + 1))
                    if j > 0:
                        act.wait_ge(ms_f_done, TT * g + j)
                    mean_square(xw_hi[:, 0:D], acc[:, j, :], ms_f[:, j:j + 1]).then_inc(ms_f_done, 1)

            def store(g):
                for j in range(TT):
                    act.wait_ge(final_done, TT * g + j + 1)
                    act.dma_start(out[g, j * P:(j + 1) * P, :], acc[:, j, :]).then_inc(stored, 16)

            def set_acc(j):
                act.dma_start(acc[:, j, :], x1[:, j, :]).then_inc(acc_set, 16)

            def load_x1(m):
                for j in range(TT):
                    act.dma_start(x1[:, j, :], xg[m, HALO + j * P:HALO + (j + 1) * P, :]).then_inc(x1_in, 16)

            load_x1(0)
            act.wait_ge(band_mid_in, 16)
            nc.scalar.copy(bm_hi[:, :, :], bm_raw[:, :, :]).then_inc(band_mid_hi, 1)
            act.wait_ge(const_set, 3)
            piece_stats(0)
            split_bands(0)
            for q in range(2):
                act.wait_ge(pool_scaled, 4 * q + 4)
                nc.scalar.copy(pw_hi[:, 4 * q:4 * q + 4, :], pw_raw[:, 4 * q:4 * q + 4, :]).then_inc(pool_hi, 1)
            split_pieces(0, 0, first=True)
            split_pooled(0, 0)
            with act.Fori(1, WINDOWS) as w:
                split_pieces(0, w)
                split_pooled(0, w)
            for h in range(2):
                act.wait_ge(wu_in, 16)
                nc.scalar.copy(wu_hi[:, h * DT // 2:(h + 1) * DT // 2, :],
                               wu_raw[:, h * DT // 2:(h + 1) * DT // 2, :]).then_inc(wu_hi_done, 1)
            mixed_stats(0, FIRST_OUTS)
            norm_mixed(0)
            for j in range(TT):
                set_acc(j)
            act.wait_ge(const_in, 96)
            for d in range(DT):
                split_h2(0, d)
            activate(0, 0, first=True)
            split_wu(1)

            def pair(n, outs):
                split_wd(n - 1, outs)
                activate(n, 1)
                split_wu(n + 1)
                split_wd(n, outs + OUTS)
                activate(n + 1, 0)
                split_wu(n + 2)

            def mix_pair(g, w, stats):
                n = CHUNKS * g + 2 * w + 1
                outs = ring_base(g) + w * MIX_PAIR_OUTS
                split_wd(n - 1, outs)
                activate(n, 1)
                split_wu(n + 1)
                if stats:
                    piece_stats(g + 1)
                split_pieces(g + 1, w)
                split_wd(n, outs + OUTS)
                split_pooled(g + 1, w)
                activate(n + 1, 0)
                split_wu(n + 2)

            with act.Fori(0, GROUPS - 1) as g:
                n0 = CHUNKS * g
                outs = ring_base(g)
                split_bands(g + 1)
                act.wait_ge(acc_set, 16 * TT * (g + 1))
                load_x1(g + 1)
                mix_pair(g, 0, True)
                with act.Fori(1, MIX_PAIRS) as w:
                    mix_pair(g, w, False)
                mixed_stats(g + 1, outs + MIX_END - OUTS)
                norm_mixed(g + 1)
                with act.Fori(0, PAIRS - 1 - MIX_PAIRS) as i:
                    pair(n0 + 2 * (i + MIX_PAIRS) + 1, outs + MIX_END + i * PAIR_OUTS)
                last = outs + GROUP_OUTS - PAIR_OUTS
                n = n0 + CHUNKS - 1
                split_wd(n - 1, last)
                activate(n, 1)
                split_h2(g + 1, 0)
                split_h2(g + 1, 1)
                split_wu(n + 1)
                for d in range(2, DT):
                    split_h2(g + 1, d)
                split_wd(n, last + OUTS)
                activate(n + 1, 0)
                split_wu(n + 2)
                final_stats(g, last + OUTS)
                store(g)
                act.wait_ge(stored, 16 * TT * (g + 1))
                for j in range(TT):
                    set_acc(j)
            n0 = CHUNKS * (GROUPS - 1)
            with act.Fori(0, PAIRS - 1) as i:
                pair(n0 + 2 * i + 1, LAST_BASE + i * PAIR_OUTS)
            last = LAST_BASE + (PAIRS - 1) * PAIR_OUTS
            split_wd(n0 + CHUNKS - 2, last)
            activate(n0 + CHUNKS - 1, 1)
            split_wd(n0 + CHUNKS - 1, last + OUTS)
            final_stats(GROUPS - 1, last + OUTS)
            store(GROUPS - 1)
            act.wait_ge(stored, 16 * TT * GROUPS)

        @block.vector
        def _(dve):
            def split_wu(n, h):
                s = slice(h * DT // 2, (h + 1) * DT // 2)
                dve.wait_ge(wu_hi_done, 2 * n + h + 1)
                nc.vector.tensor_tensor(wu_lo[:, s, :], wu_raw[:, s, :], wu_hi[:, s, :].bitcast(f32),
                                        ALU.subtract).then_inc(wu_lo_done, 1)

            def split_wd(n):
                for t in range(FT):
                    dve.wait_ge(wd_hi_done, FT * n + t + 1)
                    nc.vector.tensor_tensor(wd_lo[:, t, :], wd_raw[:, t, :], wd_hi[:, t, :].bitcast(f32),
                                            ALU.subtract).then_inc(wd_lo_done, 1)

            def split_a(n, slot, t):
                dve.wait_ge(a_hi_done, FT * n + t + 1)
                dve.wait_ge(square_done, FT * n + t + 1)
                nc.vector.tensor_tensor(a_lo[:, slot, t, :], square[:, t, :], a_hi[:, slot, t, :].bitcast(f32),
                                        ALU.subtract).then_inc(a_lo_done, 1)

            def add_down(outs, o):
                j, h = o // NH, o % NH
                dst = acc[:, j, h * HALF:(h + 1) * HALF]
                dve.wait_ge(ring_full, outs + o + 1)
                nc.vector.tensor_tensor(dst, ring_ps[:, o % RING, :], dst, ALU.add).then_inc(ring_read, 1)

            def add_pooled(m, w, outs):
                dve.wait_ge(x1_in, 16 * TT * (m + 1))
                for j in range(TT):
                    dst = x1[:, j, ds(w * WC, WC)]
                    dve.wait_ge(ring_full, outs + j + 1)
                    nc.vector.tensor_tensor(dst, ring_ps[:, j, 0:WC], dst, ALU.add).then_inc(ring_read, 1)

            def split_bands(m):
                dve.wait_ge(band_hi_done, 2 * m + 1)
                nc.vector.tensor_tensor(bf_lo[:, :, :], bf_raw[:, :, :], bf_hi[:, :, :].bitcast(f32),
                                        ALU.subtract).then_inc(band_lo_done, 1)
                dve.wait_ge(band_hi_done, 2 * m + 2)
                r = slice(0, LAST_ROWS)
                nc.vector.tensor_tensor(bl_lo[r, :, :], bl_raw[r, :, :], bl_hi[r, :, :].bitcast(f32),
                                        ALU.subtract).then_inc(band_lo_done, 1)

            def split_pieces(m, w, pieces=range(PIECES)):
                for p in pieces:
                    rows = P if p < PIECES - 1 else LAST_ROWS
                    c = slice(p * WC, (p + 1) * WC)
                    dve.wait_ge(xw_hi_done, PIECES * (WINDOWS * m + w) + p + 1)
                    nc.vector.scalar_tensor_tensor(xw_lo[0:rows, c], xp[0:rows, p, ds(w * WC, WC)],
                                                   rs_x[0:rows, p:p + 1], xw_hi[0:rows, c].bitcast(f32),
                                                   ALU.mult, ALU.subtract).then_inc(xw_lo_done, 1)

            def split_pooled(m, w, c):
                dve.wait_ge(dt_hi_done, CT * (WINDOWS * m + w) + c + 1)
                nc.vector.tensor_tensor(dt_lo[:, c, :], mix_ps[:, c, :], dt_hi[:, c, :].bitcast(f32),
                                        ALU.subtract).then_inc(dt_lo_done, 1)

            def split_h2(m, d):
                dve.wait_ge(h2_hi_done, DT * m + d + 1)
                nc.vector.scalar_tensor_tensor(h2_lo[:, d, :], mix_ps[:, d % 2, :], g_mlp_c[:, d:d + 1],
                                               h2_hi[:, d, :].bitcast(f32),
                                               ALU.mult, ALU.subtract).then_inc(h2_lo_done, 1)

            def finish(g, j):
                dve.wait_ge(rs_f_done, TT * g + j + 1)
                nc.vector.scalar_tensor_tensor(acc[:, j, :], acc[:, j, :], rs_f[:, j:j + 1], g_fin_b[:, :],
                                               ALU.mult, ALU.mult).then_inc(final_done, 1)

            nc.vector.memset(power[:, :], -0.5).then_inc(const_set, 1)
            nc.vector.memset(eps[:, :], EPS).then_inc(const_set, 1)
            nc.vector.memset(ms_x[:, :], 1.0).then_inc(const_set, 1)
            dve.wait_ge(const_in, 96)
            for q in range(WINDOWS * CT):
                nc.vector.scalar_tensor_tensor(pw_raw[:, q, :], pw_raw[:, q, :], g_mix_c[:, q:q + 1],
                                               scale_b[:, (q // CT) * WC:(q // CT + 1) * WC],
                                               ALU.mult, ALU.mult).then_inc(pool_scaled, 1)
            split_bands(0)
            for q in range(2):
                s = slice(4 * q, 4 * q + 4)
                dve.wait_ge(pool_hi, q + 1)
                nc.vector.tensor_tensor(pw_lo[:, s, :], pw_raw[:, s, :], pw_hi[:, s, :].bitcast(f32),
                                        ALU.subtract).then_inc(pool_lo, 1)
            with dve.Fori(0, WINDOWS) as w:
                split_pieces(0, w)
                for c in range(CT):
                    split_pooled(0, w, c)
                add_pooled(0, w, w * TT)
            split_wu(0, 0)
            split_wu(0, 1)
            for d in range(DT):
                split_h2(0, d)
            split_a(0, 0, 0)
            split_a(0, 0, 1)
            split_wu(1, 0)
            split_wu(1, 1)

            def step_down(n, slot, outs):
                split_a(n, slot, 1)
                for o in range(OUTS):
                    add_down(outs, o)
                    if o < 2:
                        split_wu(n + 1, o)

            with dve.Fori(0, GROUPS - 1) as g:
                n0 = CHUNKS * g
                outs = ring_base(g)
                split_bands(g + 1)
                with dve.Fori(0, MIX_PAIRS) as w:
                    n = n0 + 2 * w + 1
                    outs_w = outs + w * MIX_PAIR_OUTS
                    split_wd(n - 1)
                    split_a(n, 1, 0)
                    split_a(n, 1, 1)
                    dve.wait_ge(acc_set, 16 * TT * (g + 1))
                    for o in range(OUTS):
                        add_down(outs_w, o)
                        if o < 2:
                            split_wu(n + 1, o)
                        if o >= OUTS - PIECES:
                            split_pieces(g + 1, w, [o - (OUTS - PIECES)])
                    for c in range(CT):
                        split_pooled(g + 1, w, c)
                    split_wd(n)
                    split_a(n + 1, 0, 0)
                    add_pooled(g + 1, w, outs_w + OUTS)
                    step_down(n + 1, 0, outs_w + OUTS + TT)
                with dve.Fori(0, PAIRS - 1 - MIX_PAIRS) as i:
                    n = n0 + 2 * (i + MIX_PAIRS) + 1
                    outs_i = outs + MIX_END + i * PAIR_OUTS
                    split_wd(n - 1)
                    split_a(n, 1, 0)
                    step_down(n, 1, outs_i)
                    split_wd(n)
                    split_a(n + 1, 0, 0)
                    step_down(n + 1, 0, outs_i + OUTS)
                n = n0 + CHUNKS - 1
                last = outs + GROUP_OUTS - PAIR_OUTS
                split_wd(n - 1)
                split_a(n, 1, 0)
                split_a(n, 1, 1)
                split_h2(g + 1, 0)
                split_h2(g + 1, 1)
                for o in range(OUTS):
                    add_down(last, o)
                    if o < 2:
                        split_wu(n + 1, o)
                    if o + 2 < DT:
                        split_h2(g + 1, o + 2)
                split_wd(n)
                split_a(n + 1, 0, 0)
                split_a(n + 1, 0, 1)
                for o in range(OUTS):
                    add_down(last + OUTS, o)
                    if o < 2:
                        split_wu(n + 2, o)
                    if o % NH == NH - 1 and o >= 2 * NH - 1:
                        finish(g, o // NH - 1)
                finish(g, TT - 1)
            n0 = CHUNKS * (GROUPS - 1)
            dve.wait_ge(acc_set, 16 * TT * GROUPS)
            with dve.Fori(0, PAIRS - 1) as i:
                n = n0 + 2 * i + 1
                outs_i = LAST_BASE + i * PAIR_OUTS
                split_wd(n - 1)
                split_a(n, 1, 0)
                step_down(n, 1, outs_i)
                split_wd(n)
                split_a(n + 1, 0, 0)
                step_down(n + 1, 0, outs_i + OUTS)
            n = n0 + CHUNKS - 1
            last = LAST_BASE + (PAIRS - 1) * PAIR_OUTS
            split_wd(n - 1)
            split_a(n, 1, 0)
            split_a(n, 1, 1)
            for o in range(OUTS):
                add_down(last, o)
            split_wd(n)
            for o in range(OUTS):
                add_down(last + OUTS, o)
                if o % NH == NH - 1 and o >= 2 * NH - 1:
                    finish(GROUPS - 1, o // NH - 1)
            finish(GROUPS - 1, TT - 1)

        @block.gpsimd
        def _(pool):
            def squares(n, first=False):
                for t in range(FT):
                    pool.wait_ge(relu_done, FT * n + t + 1)
                    if not first:
                        pool.wait_ge(a_lo_done, FT * (n - 1) + t + 1)
                    nc.gpsimd.tensor_tensor(square[:, t, :], relu[:, t, :], relu[:, t, :],
                                            ALU.mult).then_inc(square_done, 1)

            def rms(ms, me, rs, width, me_sem, count, rs_sem):
                nc.gpsimd.tensor_tensor(me, ms, eps[:, 0:width], ALU.add).then_inc(me_sem, 1)
                pool.wait_ge(me_sem, count)
                nc.gpsimd.tensor_tensor(rs, me, power[:, 0:width], ALU.pow).then_inc(rs_sem, 1)

            def piece_rms(m):
                pool.wait_ge(ms_x_done, PIECES * (m + 1))
                rms(ms_x[:, :], me_x[:, :], rs_x[:, :], PIECES, me_x_done, m + 1, rs_x_done)

            def mixed_rms(m):
                pool.wait_ge(ms_m_done, TT * (m + 1))
                rms(ms_m[:, :], me_m[:, :], rs_m[:, :], TT, me_m_done, m + 1, rs_m_done)

            def final_rms(g):
                for j in range(TT):
                    c = slice(j, j + 1)
                    pool.wait_ge(ms_f_done, TT * g + j + 1)
                    rms(ms_f[:, c], me_f[:, c], rs_f[:, c], 1, me_f_done, TT * g + j + 1, rs_f_done)

            pool.wait_ge(const_set, 3)
            piece_rms(0)
            mixed_rms(0)
            squares(0, first=True)
            with pool.Fori(0, GROUPS - 1) as g:
                n0 = CHUNKS * g
                squares(n0 + 1)
                piece_rms(g + 1)
                with pool.Fori(1, 2 * MIX_PAIRS) as i:
                    squares(n0 + i + 1)
                mixed_rms(g + 1)
                with pool.Fori(2 * MIX_PAIRS, CHUNKS) as i:
                    squares(n0 + i + 1)
                final_rms(g)
            n0 = CHUNKS * (GROUPS - 1)
            with pool.Fori(1, CHUNKS) as i:
                squares(n0 + i)
            final_rms(GROUPS - 1)

        @block.tensor
        def _(pe):
            def up(n, first=False):
                for t in range(FT):
                    c = slice(t * P, (t + 1) * P)
                    if not first:
                        pe.wait_ge(relu_done, FT * (n - 1) + t + 1)
                    for d in range(DT):
                        if t == 0 and d % (DT // 2) == 0:
                            pe.wait_ge(wu_lo_done, 2 * n + d // (DT // 2) + 1)
                        o = up_ps[:, t, :]
                        nc.tensor.matmul(o, wu_hi[:, d, c], h2_hi[:, d, :], start=(d == 0), stop=False)
                        nc.tensor.matmul(o, wu_hi[:, d, c], h2_lo[:, d, :], start=False, stop=False)
                        last = nc.tensor.matmul(o, wu_lo[:, d, c], h2_hi[:, d, :], start=False, stop=(d == DT - 1))
                    last.then_inc(up_done, 1)

            def down_out(slot, outs, o):
                j, h = o // NH, o % NH
                r = slice(j * P, (j + 1) * P)
                c = slice(h * HALF, (h + 1) * HALF)
                pe.wait_ge(ring_read, outs + o + 1 - RING)
                dst = ring_ps[:, o % RING, :]
                for t in range(FT):
                    nc.tensor.matmul(dst, a_hi[:, slot, t, r], wd_hi[:, t, c], start=(t == 0), stop=False)
                    nc.tensor.matmul(dst, a_hi[:, slot, t, r], wd_lo[:, t, c], start=False, stop=False)
                    last = nc.tensor.matmul(dst, a_lo[:, slot, t, r], wd_hi[:, t, c],
                                            start=False, stop=(t == FT - 1))
                last.then_inc(ring_full, 1)

            def down_ready(n):
                pe.wait_ge(wd_lo_done, FT * (n + 1))
                pe.wait_ge(a_lo_done, FT * (n + 1))

            def down(n, slot, outs):
                down_ready(n)
                for o in range(OUTS):
                    down_out(slot, outs, o)

            def pool_window(m, w, first=False):
                pe.wait_ge(xw_lo_done, PIECES * (WINDOWS * m + w + 1))
                for c in range(CT):
                    if not first:
                        pe.wait_ge(dt_lo_done, CT * (WINDOWS * m + w - 1) + c + 1)
                    for p in range(PIECES):
                        rows, width = (P, PIECE) if p < PIECES - 1 else (LAST_ROWS, LAST)
                        ch = slice(p * WC + c * P, p * WC + (c + 1) * P)
                        hi, lo = (bf_hi, bf_lo) if p == 0 else (bl_hi, bl_lo) if p == PIECES - 1 else (bm_hi, None)
                        o = mix_ps[:, c, p * PIECE:p * PIECE + width]
                        nc.tensor.matmul(o, xw_hi[0:rows, ch], hi[0:rows, w, :], start=True, stop=False)
                        last = nc.tensor.matmul(o, xw_lo[0:rows, ch], hi[0:rows, w, :],
                                                start=False, stop=(lo is None))
                        if lo is not None:
                            last = nc.tensor.matmul(o, xw_hi[0:rows, ch], lo[0:rows, w, :], start=False, stop=True)
                    last.then_inc(pooled, 1)

            def pool_out(m, w, outs, first=False):
                pe.wait_ge(dt_lo_done, CT * (WINDOWS * m + w + 1))
                for j in range(TT):
                    r = slice(j * P, (j + 1) * P)
                    if not first:
                        pe.wait_ge(ring_read, outs + j + 1 - RING)
                    dst = ring_ps[:, j, 0:WC]
                    for c in range(CT):
                        q = w * CT + c
                        nc.tensor.matmul(dst, dt_hi[:, c, r], pw_hi[:, q, :], start=(c == 0), stop=False)
                        nc.tensor.matmul(dst, dt_hi[:, c, r], pw_lo[:, q, :], start=False, stop=False)
                        last = nc.tensor.matmul(dst, dt_lo[:, c, r], pw_hi[:, q, :], start=False, stop=(c == CT - 1))
                    last.then_inc(ring_full, 1)

            def transpose(m, d):
                if d < 2:
                    pe.wait_ge(dt_lo_done, CT * WINDOWS * (m + 1))
                else:
                    pe.wait_ge(h2_lo_done, DT * m + d - 1)
                for j in range(TT):
                    last = nc.tensor.transpose(mix_ps[:, d % 2, j * P:(j + 1) * P],
                                               xp[:, j, d * P:(d + 1) * P], ident[:, :])
                last.then_inc(transposed, 1)

            pe.wait_ge(band_mid_hi, 1)
            pe.wait_ge(band_lo_done, 2)
            pool_window(0, 0, first=True)
            pe.wait_ge(pool_lo, 2)
            pool_out(0, 0, 0, first=True)
            with pe.Fori(1, WINDOWS) as w:
                pool_window(0, w)
                pool_out(0, w, w * TT)
            pe.wait_ge(const_in, 96)
            pe.wait_ge(x1n_done, TT)
            for d in range(DT):
                transpose(0, d)
            pe.wait_ge(h2_lo_done, DT)
            up(0, first=True)

            with pe.Fori(0, GROUPS - 1) as g:
                n0 = CHUNKS * g
                outs = ring_base(g)
                with pe.Fori(0, MIX_PAIRS) as w:
                    n = n0 + 2 * w + 1
                    outs_w = outs + w * MIX_PAIR_OUTS
                    up(n)
                    down(n - 1, 0, outs_w)
                    pe.wait_ge(band_lo_done, 2 * (g + 2))
                    pe.wait_ge(h2_lo_done, DT * (g + 1))
                    pool_window(g + 1, w)
                    up(n + 1)
                    pool_out(g + 1, w, outs_w + OUTS)
                    down(n, 1, outs_w + OUTS + TT)
                with pe.Fori(0, PAIRS - 1 - MIX_PAIRS) as i:
                    n = n0 + 2 * (i + MIX_PAIRS) + 1
                    outs_i = outs + MIX_END + i * PAIR_OUTS
                    up(n)
                    down(n - 1, 0, outs_i)
                    up(n + 1)
                    down(n, 1, outs_i + OUTS)
                n = n0 + CHUNKS - 1
                last = outs + GROUP_OUTS - PAIR_OUTS
                up(n)
                down_ready(n - 1)
                pe.wait_ge(x1n_done, TT * (g + 2))
                transpose(g + 1, 0)
                transpose(g + 1, 1)
                for o in range(OUTS):
                    down_out(0, last, o)
                    if o + 2 < DT:
                        transpose(g + 1, o + 2)
                pe.wait_ge(h2_lo_done, DT * (g + 2))
                up(n + 1)
                down(n, 1, last + OUTS)
            n0 = CHUNKS * (GROUPS - 1)
            with pe.Fori(0, PAIRS - 1) as i:
                n = n0 + 2 * i + 1
                outs_i = LAST_BASE + i * PAIR_OUTS
                up(n)
                down(n - 1, 0, outs_i)
                up(n + 1)
                down(n, 1, outs_i + OUTS)
            n = n0 + CHUNKS - 1
            last = LAST_BASE + (PAIRS - 1) * PAIR_OUTS
            up(n)
            down(n - 1, 0, last)
            down(n, 1, last + OUTS)


def bands():
    import numpy as np

    def band(win, rows, width, lo_row, hi_row):
        b = np.zeros((rows, width), np.float64)
        for t in range(width):
            a, e = max(t + HALO - win // 2, lo_row), min(t + HALO + win // 2, hi_row)
            b[a:e, t] = 1.0 / (e - a)
            b[t + HALO, t] -= 1.0
        return b

    wins = (2, 4, 8, 16)
    starts, ends = (0, GROUPS - 1), (GROUPS - 2, GROUPS - 1)
    mid = np.stack([band(w, P, PIECE, 0, P) for w in wins], 1)
    first = np.stack([np.stack([band(w, P, PIECE, HALO if g in starts else 0, P) for w in wins], 1)
                      for g in range(GROUPS)])
    last = np.stack([np.stack([band(w, LAST_ROWS, LAST, 0, LAST + HALO if g in ends else LAST_ROWS)
                               for w in wins], 1) for g in range(GROUPS)])
    return first.astype(np.float32), mid.astype(np.float32), last.astype(np.float32)


def kernel(x_prompt, x_sample, norm_mix_g, norm_mlp_g, w_up, w_down, final_norm_g, pool_w, pool_scale, **unused):
    import concourse.bacc as bacc
    import numpy as np
    from concourse.bass_utils import run_bass_kernel_spmd

    xp, xs = np.asarray(x_prompt)[0], np.asarray(x_sample)[0]
    xg = np.zeros((GROUPS, XROWS, D), np.float32)
    for seq, g0 in ((xp, 0), (xs, GROUPS - 1)):
        for g in range(len(seq) // GT):
            a, e = max(g * GT - HALO, 0), min((g + 1) * GT + HALO, len(seq))
            xg[g0 + g, a - g * GT + HALO:e - g * GT + HALO] = seq[a:e]
    first, mid, last = bands()
    arrays = {
        "xg": xg,
        "w_up": np.ascontiguousarray(np.asarray(w_up)[0]),
        "w_down": np.ascontiguousarray(np.asarray(w_down)[0]),
        "pool_w": np.ascontiguousarray(np.asarray(pool_w)[0]),
        "pool_scale": np.ascontiguousarray(np.asarray(pool_scale)[0]),
        "g_mix": np.ascontiguousarray(np.asarray(norm_mix_g)[0].reshape(DT, P).T),
        "g_mlp": np.ascontiguousarray(np.asarray(norm_mlp_g)[0].reshape(DT, P).T),
        "g_fin": np.ascontiguousarray(np.asarray(final_norm_g)),
        "band_first": first,
        "band_mid": mid,
        "band_last": last,
        "ident_in": np.eye(P, dtype=np.float32),
    }
    nc = bacc.Bacc("TRN2", target_bir_lowering=False, num_devices=1)
    args = [nc.dram_tensor(name, a.shape, mybir.dt.float32, kind="ExternalInput").ap() for name, a in arrays.items()]
    out = nc.dram_tensor("out", (GROUPS, GT, D), mybir.dt.float32, kind="ExternalOutput").ap()
    build(nc, *args, out)
    r = run_bass_kernel_spmd(nc, [arrays], core_ids=[0])
    y = r.results[0]["out"].reshape(1, GROUPS * GT, D)
    n = xp.shape[0]
    return y[:, :n], y[:, n:]
```

```python
from contextlib import ExitStack

import concourse.bass as bass
from concourse import mybir
from concourse.alu_op_type import AluOpType as ALU

P = 128
D = 1024
F = 4096
GT = 512
GROUPS = 5
EPS = 1e-6
WINDOWS = 4
WC = D // WINDOWS
CT = WC // P
HALO = 8
HT = GT + 2 * HALO
NORMS = GT // P + 1
FC = 256
CHUNKS = F // FC
FT = FC // P
DT = D // P
TT = GT // P
HALF = 512
NH = D // HALF
OUTS = TT * NH
RING = 4
MIX_PAIRS = WINDOWS
PAIRS = CHUNKS // 2
PAIR_OUTS = 2 * OUTS
MIX_PAIR_OUTS = PAIR_OUTS + TT
GROUP_OUTS = PAIRS * PAIR_OUTS + WINDOWS * TT
ACC_LOADS = 2 * 16
FIRST_OUTS = WINDOWS * TT
TURNS = CT + 1
SUM_STEPS = [sum(v + 2 for v in range(w)) for w in range(WINDOWS + 1)]


def build(nc, x, halos, w_up, w_down, pool_w, pool_scale, g_mix, g_mlp, g_fin, ends, ident_in, out):
    f32 = mybir.dt.float32
    f32r = mybir.dt.float32r
    ACT = mybir.ActivationFunctionType
    ds = bass.ds

    w_up_v = w_up.rearrange("(t p) f -> p t f", p=P)
    w_down_v = w_down.rearrange("(t p) d -> p t d", p=P)
    pool_w_v = pool_w.rearrange("g (t p) e -> p (g t) e", p=P)

    ctx = ExitStack()
    with ctx:
        def sb(name, shape, dt=f32):
            return ctx.enter_context(nc.sbuf_tensor(name, shape, dt))

        def pb(name, shape):
            return ctx.enter_context(nc.psum_tensor(name, shape, f32))

        def sem(name):
            return ctx.enter_context(nc.semaphore(name))

        h2_hi = sb("h2_hi", [P, DT, GT], f32r)
        h2_lo = sb("h2_lo", [P, DT, GT], f32r)
        wu_raw = sb("wu_raw", [P, DT, FC])
        wu_hi = sb("wu_hi", [P, DT, FC], f32r)
        wu_lo = sb("wu_lo", [P, DT, FC], f32r)
        wd_raw = sb("wd_raw", [P, FT, D])
        wd_hi = sb("wd_hi", [P, FT, D], f32r)
        wd_lo = sb("wd_lo", [P, FT, D], f32r)
        relu = sb("relu", [P, FT, GT])
        square = sb("square", [P, FT, GT])
        a_hi = sb("a_hi", [P, 2, FT, GT], f32r)
        a_lo = sb("a_lo", [P, 2, FT, GT], f32r)
        wd_last_hi = h2_hi[:, 0:FT * NH, :]
        wd_last_lo = h2_lo[:, 0:FT * NH, :]
        acc = sb("acc", [P, TT, D])
        xr = sb("xr", [P, TT, D])
        xh = sb("xh", [2 * HALO, D])
        xw = sb("xw", [P, NORMS, WC])
        ht = sb("ht", [P, CT, HT])
        sums = [sb(f"sums{i}", [P, CT, HT]) for i in range(2)]
        end_scale = sb("end_scale", [P, WINDOWS, CT, 2, HALO])
        dt_hi = sb("dt_hi", [P, CT, GT], f32r)
        dt_lo = sb("dt_lo", [P, CT, GT], f32r)
        junk = dt_hi[:, :, :].rearrange("p c t -> p (c t)")
        x1 = sb("x1", [P, TT, D])
        pw_hi = sb("pw_hi", [P, WINDOWS * CT, WC], f32r)
        pw_lo = sb("pw_lo", [P, WINDOWS * CT, WC], f32r)
        g_fin_b = sb("g_fin_b", [P, D])
        g_mix_c = sb("g_mix_c", [P, DT])
        g_mlp_c = sb("g_mlp_c", [P, DT])
        ident = sb("ident", [P, P])
        power = sb("power", [P, NORMS])
        eps = sb("eps", [P, NORMS])
        ms_x = sb("ms_x", [P, NORMS])
        me_x = sb("me_x", [P, NORMS])
        rs_x = sb("rs_x", [P, NORMS])
        ms_m = sb("ms_m", [P, TT])
        me_m = sb("me_m", [P, TT])
        rs_m = sb("rs_m", [P, TT])
        ms_f = sb("ms_f", [P, TT])
        me_f = sb("me_f", [P, TT])
        rs_f = sb("rs_f", [P, TT])
        pw_raw = acc[:, 0:2, :].rearrange("p a (b e) -> p (a b) e", e=WC)
        scale_b = acc[:, 2, :]

        up_ps = pb("up_ps", [P, FT, HALF])
        ring_ps = pb("ring_ps", [P, RING, HALF])
        mix_ps = pb("mix_ps", [P, 2, HALF])

        acc_moved = sem("acc_moved")
        g_mix_in = sem("g_mix_in")
        gain_in = sem("gain_in")
        const_set = sem("const_set")
        pool_scaled = sem("pool_scaled")
        pool_hi = sem("pool_hi")
        pool_lo = sem("pool_lo")
        wu_in = sem("wu_in")
        wu_hi_done = sem("wu_hi_done")
        wu_lo_done = sem("wu_lo_done")
        wd_in = sem("wd_in")
        wd_hi_done = sem("wd_hi_done")
        wd_lo_done = sem("wd_lo_done")
        up_done = sem("up_done")
        relu_done = sem("relu_done")
        square_done = sem("square_done")
        a_hi_done = sem("a_hi_done")
        a_lo_done = sem("a_lo_done")
        ring_full = sem("ring_full")
        ring_read = sem("ring_read")
        xr_in = [sem(f"xr_in{j}") for j in range(TT)]
        halo_in = sem("halo_in")
        ends_in = sem("ends_in")
        ms_x_done = sem("ms_x_done")
        me_x_done = sem("me_x_done")
        rs_x_done = sem("rs_x_done")
        xw_done = sem("xw_done")
        x_turned = sem("x_turned")
        ht_done = sem("ht_done")
        summed = sem("summed")
        diff_done = sem("diff_done")
        dt_hi_done = sem("dt_hi_done")
        dt_lo_done = sem("dt_lo_done")
        ms_m_done = sem("ms_m_done")
        me_m_done = sem("me_m_done")
        rs_m_done = sem("rs_m_done")
        x1n_done = sem("x1n_done")
        transposed = sem("transposed")
        h2_hi_done = sem("h2_hi_done")
        h2_lo_done = sem("h2_lo_done")
        ms_f_done = sem("ms_f_done")
        me_f_done = sem("me_f_done")
        rs_f_done = sem("rs_f_done")
        final_done = sem("final_done")

        block = ctx.enter_context(nc.Block())

        def ring_base(g):
            return FIRST_OUTS + g * GROUP_OUTS

        LAST_BASE = ring_base(GROUPS - 1)
        MIX_END = MIX_PAIRS * MIX_PAIR_OUTS

        def window_sums(engine, eng, m, w):
            eng.wait_ge(ends_in, 16 * (m + 1))
            eng.wait_ge(ht_done, TURNS * (WINDOWS * m + w + 1))
            done = SUM_STEPS[WINDOWS] * m + SUM_STEPS[w]
            src = ht
            for level in range(w + 1):
                shift = 2 ** level
                last = level == w
                first = HALO - 2 ** w
                n = GT + 2 ** (w + 1) - 2 * shift
                dst, to = sums[level % 2], (2 ** w if last else 0)
                engine.tensor_tensor(dst[:, :, first + to:first + to + n], src[:, :, first:first + n],
                                     src[:, :, first + shift:first + shift + n], ALU.add).then_inc(summed, 1)
                done = done + 1
                eng.wait_ge(summed, done)
                src = dst
            ends_of = src[:, :, HALO:HALO + GT].rearrange("p c (a b) -> p c a b", b=HALO)
            both = ends_of[:, :, 0:GT // HALO:GT // HALO - 1, :]
            engine.tensor_tensor(both, both, end_scale[:, w, :, :, :], ALU.mult).then_inc(summed, 1)

        @block.sync
        def _(sp):
            def load_wu(n, k):
                sp.dma_start(wu_raw[:, :, :], w_up_v[:, :, ds(k * FC, FC)]).then_inc(wu_in, 16)

            def load_wd(n, k):
                sp.dma_start(wd_raw[:, :, :], w_down_v[:, ds(k * FT, FT), :]).then_inc(wd_in, 16)

            def step(n, k, k_next):
                sp.wait_ge(wu_lo_done, 2 * n + 2)
                load_wu(n + 1, k_next)
                sp.wait_ge(wd_lo_done, 2 * n)
                load_wd(n, k)

            def load_rows(m):
                for j in range(TT):
                    sp.dma_start(xr[:, j, :], x[m, j * P:(j + 1) * P, :]).then_inc(xr_in[j], 16)

            def load_halos(m):
                sp.dma_start(xh[:, :], halos[m]).then_inc(halo_in, 16)

            def load_ends(m):
                sp.dma_start(end_scale[:, :, :, :, :], ends[m]).then_inc(ends_in, 16)

            def store(g):
                for j in range(TT):
                    sp.wait_ge(final_done, TT * g + j + 1)
                    sp.dma_start(out[g, j * P:(j + 1) * P, :], acc[:, j, :]).then_inc(acc_moved, 16)

            def prefetch_rows(m):
                sp.wait_ge(transposed, DT * m)
                load_rows(m)
                sp.wait_ge(xw_done, NORMS * WINDOWS * m)
                load_halos(m)
                sp.wait_ge(summed, SUM_STEPS[WINDOWS] * m)
                load_ends(m)

            load_rows(0)
            load_halos(0)
            load_ends(0)
            sp.dma_start(pw_raw, pool_w_v).then_inc(acc_moved, 16)
            sp.dma_start(scale_b, pool_scale.partition_broadcast(P)).then_inc(acc_moved, 16)
            sp.dma_start(g_mix_c[:, :], g_mix).then_inc(g_mix_in, 16)
            sp.dma_start(g_mlp_c[:, :], g_mlp).then_inc(gain_in, 16)
            sp.dma_start(ident[:, :], ident_in).then_inc(gain_in, 16)
            sp.dma_start(g_fin_b[:, :], g_fin.partition_broadcast(P)).then_inc(gain_in, 16)
            load_wu(0, 0)
            load_wd(0, 0)
            sp.wait_ge(wu_lo_done, 2)
            load_wu(1, 1)
            prefetch_rows(1)
            sp.wait_ge(wu_lo_done, 4)
            load_wu(2, 2)

            def group(g, mixer, prefetch):
                n0 = CHUNKS * g
                sp.wait_ge(wd_lo_done, 2 * (n0 + 1))
                load_wd(n0 + 1, 1)
                with sp.Fori(2, CHUNKS - 1) as k:
                    step(n0 + k, k, k + 1)
                if mixer:
                    step(n0 + CHUNKS - 1, CHUNKS - 1, 0)
                    step(n0 + CHUNKS, 0, 1)
                else:
                    sp.wait_ge(wd_lo_done, 2 * (n0 + CHUNKS - 1))
                    load_wd(n0 + CHUNKS - 1, CHUNKS - 1)
                if prefetch:
                    prefetch_rows(g + 2)
                if mixer:
                    sp.wait_ge(wu_lo_done, 2 * (n0 + CHUNKS + 2))
                    load_wu(n0 + CHUNKS + 2, 2)
                store(g)

            with sp.Fori(0, GROUPS - 2) as g:
                group(g, True, True)
            group(GROUPS - 2, True, False)
            group(GROUPS - 1, False, False)
            sp.wait_ge(acc_moved, ACC_LOADS + 16 * TT * GROUPS)

        @block.scalar
        def _(act):
            def split_wu(n):
                for h in range(2):
                    act.wait_ge(wu_in, 16 * (n + 1))
                    act.wait_ge(up_done, FT * n)
                    s = slice(h * DT // 2, (h + 1) * DT // 2)
                    nc.scalar.copy(wu_hi[:, s, :], wu_raw[:, s, :]).then_inc(wu_hi_done, 1)

            def split_wd(n, outs_before):
                for t in range(FT):
                    act.wait_ge(wd_in, 16 * (n + 1))
                    act.wait_ge(ring_full, outs_before)
                    nc.scalar.copy(wd_hi[:, t, :], wd_raw[:, t, :]).then_inc(wd_hi_done, 1)

            def activate(n, slot, first=False):
                for t in range(FT):
                    act.wait_ge(up_done, FT * n + t + 1)
                    if not first:
                        act.wait_ge(square_done, FT * (n - 1) + t + 1)
                    nc.scalar.activation(relu[:, t, :], up_ps[:, t, :], ACT.Relu).then_inc(relu_done, 1)
                    act.wait_ge(relu_done, FT * n + t + 1)
                    nc.scalar.activation(a_hi[:, slot, t, :], relu[:, t, :], ACT.Square).then_inc(a_hi_done, 1)

            def mean_square(src, dst, rows=P):
                return nc.scalar.activation(junk[0:rows, :], src, ACT.Square, scale=D ** -0.5, accum_out=dst)

            def row_stats(m):
                for j in range(NORMS):
                    act.wait_ge(xr_in[j] if j < TT else halo_in, 16 * (m + 1))
                    if j > 0:
                        act.wait_ge(ms_x_done, NORMS * m + j)
                    rows, src = (P, xr[:, j, :]) if j < TT else (2 * HALO, xh[:, :])
                    mean_square(src, ms_x[0:rows, j:j + 1], rows).then_inc(ms_x_done, 1)

            def norm_rows(m, w):
                act.wait_ge(rs_x_done, m + 1)
                for j in range(NORMS):
                    rows, src = (P, xr[:, j, ds(w * WC, WC)]) if j < TT else (2 * HALO, xh[:, ds(w * WC, WC)])
                    nc.scalar.activation(xw[0:rows, j, :], src, ACT.Copy,
                                         scale=rs_x[0:rows, j:j + 1]).then_inc(xw_done, 1)

            def next_norm_rows(m, w):
                act.wait_ge(x_turned, TURNS * (WINDOWS * m + w))
                norm_rows(m, w)

            def keep_turned(m, w):
                v = WINDOWS * m + w
                for c in range(CT):
                    act.wait_ge(x_turned, TURNS * v + c + 1)
                    nc.scalar.copy(ht[:, c, HALO:HALO + GT], mix_ps[:, c, :]).then_inc(ht_done, 1)
                act.wait_ge(x_turned, TURNS * v + TURNS)
                both = ht[:, :, :].rearrange("p c (a b) -> p c a b", b=HALO)[:, :, 0:HT // HALO:HT // HALO - 1, :]
                src = mix_ps[:, 0, 0:CT * P].rearrange("p (c a b) -> p c a b", c=CT, b=HALO)[:, :, 0:2, :]
                nc.scalar.copy(both, src).then_inc(ht_done, 1)

            def split_pooled(m, w):
                act.wait_ge(diff_done, WINDOWS * m + w + 1)
                nc.scalar.copy(dt_hi[:, :, :], sums[w % 2][:, :, HALO:HALO + GT]).then_inc(dt_hi_done, 1)

            def mixed_stats(m, outs):
                act.wait_ge(ring_read, outs)
                for j in range(TT):
                    if j > 0:
                        act.wait_ge(ms_m_done, TT * m + j)
                    mean_square(x1[:, j, :], ms_m[:, j:j + 1]).then_inc(ms_m_done, 1)

            def norm_mixed(m):
                act.wait_ge(rs_m_done, m + 1)
                for j in range(TT):
                    nc.scalar.activation(xr[:, j, :], x1[:, j, :], ACT.Copy,
                                         scale=rs_m[:, j:j + 1]).then_inc(x1n_done, 1)

            def split_h2(m, d):
                act.wait_ge(transposed, DT * m + d + 1)
                nc.scalar.activation(h2_hi[:, d, :], mix_ps[:, d % 2, :], ACT.Copy,
                                     scale=g_mlp_c[:, d:d + 1]).then_inc(h2_hi_done, 1)

            def final_stats(g, outs_before):
                for j in range(TT):
                    act.wait_ge(ring_read, outs_before + NH * (j + 1))
                    if j > 0:
                        act.wait_ge(ms_f_done, TT * g + j)
                    mean_square(acc[:, j, :], ms_f[:, j:j + 1]).then_inc(ms_f_done, 1)

            act.wait_ge(const_set, 4)
            row_stats(0)
            norm_rows(0, 0)
            for w in range(WINDOWS):
                if w > 0:
                    act.wait_ge(diff_done, w)
                keep_turned(0, w)
                if w + 1 < WINDOWS:
                    next_norm_rows(0, w + 1)
                if w == 0:
                    for q in range(2):
                        act.wait_ge(pool_scaled, 4 * q + 4)
                        nc.scalar.copy(pw_hi[:, 4 * q:4 * q + 4, :],
                                       pw_raw[:, 4 * q:4 * q + 4, :]).then_inc(pool_hi, 1)
                else:
                    act.wait_ge(ring_full, TT * w)
                split_pooled(0, w)
            for h in range(2):
                act.wait_ge(wu_in, 16)
                nc.scalar.copy(wu_hi[:, h * DT // 2:(h + 1) * DT // 2, :],
                               wu_raw[:, h * DT // 2:(h + 1) * DT // 2, :]).then_inc(wu_hi_done, 1)
            mixed_stats(0, FIRST_OUTS)
            norm_mixed(0)
            act.wait_ge(gain_in, 48)
            for d in range(DT):
                split_h2(0, d)
            activate(0, 0, first=True)
            split_wu(1)

            def pair(n, outs):
                split_wd(n - 1, outs)
                activate(n, 1)
                split_wu(n + 1)
                split_wd(n, outs + OUTS)
                activate(n + 1, 0)
                split_wu(n + 2)

            def mix_pair(g, w):
                n = CHUNKS * g + 2 * w + 1
                outs = ring_base(g) + w * MIX_PAIR_OUTS
                split_wd(n - 1, outs)
                if w == 0:
                    row_stats(g + 1)
                activate(n, 1)
                split_wu(n + 1)
                next_norm_rows(g + 1, w)
                act.wait_ge(dt_lo_done, WINDOWS * (g + 1) + w)
                keep_turned(g + 1, w)
                split_wd(n, outs + OUTS)
                activate(n + 1, 0)
                split_wu(n + 2)
                split_pooled(g + 1, w)

            with act.Fori(0, GROUPS - 1) as g:
                n0 = CHUNKS * g
                outs = ring_base(g)
                for w in range(MIX_PAIRS):
                    mix_pair(g, w)
                n = n0 + 2 * MIX_PAIRS + 1
                split_wd(n - 1, outs + MIX_END)
                activate(n, 1)
                split_wu(n + 1)
                mixed_stats(g + 1, outs + MIX_END)
                norm_mixed(g + 1)
                split_wd(n, outs + MIX_END + OUTS)
                activate(n + 1, 0)
                split_wu(n + 2)
                with act.Fori(1, PAIRS - 1 - MIX_PAIRS) as i:
                    pair(n0 + 2 * (i + MIX_PAIRS) + 1, outs + MIX_END + i * PAIR_OUTS)
                last = outs + GROUP_OUTS - PAIR_OUTS
                n = n0 + CHUNKS - 1
                split_wd(n - 1, last)
                activate(n, 1)
                split_h2(g + 1, 0)
                split_h2(g + 1, 1)
                split_wu(n + 1)
                for d in range(2, DT):
                    split_h2(g + 1, d)
                split_wd(n, last + OUTS)
                activate(n + 1, 0)
                split_wu(n + 2)
                final_stats(g, last + OUTS)
                act.wait_ge(ms_f_done, TT * (g + 1))
            n0 = CHUNKS * (GROUPS - 1)
            with act.Fori(0, PAIRS - 1) as i:
                pair(n0 + 2 * i + 1, LAST_BASE + i * PAIR_OUTS)
            last = LAST_BASE + (PAIRS - 1) * PAIR_OUTS
            split_wd(n0 + CHUNKS - 2, last)
            activate(n0 + CHUNKS - 1, 1)
            n = n0 + CHUNKS - 1
            for t in range(FT):
                act.wait_ge(wd_in, 16 * (n + 1))
                act.wait_ge(up_done, FT * (n + 1))
                nc.scalar.copy(wd_last_hi[:, NH * t:NH * (t + 1), :],
                               wd_raw[:, t, :].rearrange("p (h e) -> p h e", h=NH)).then_inc(wd_hi_done, 1)
            final_stats(GROUPS - 1, last + OUTS)

        @block.vector
        def _(dve):
            def split_wu(n, h):
                s = slice(h * DT // 2, (h + 1) * DT // 2)
                dve.wait_ge(wu_hi_done, 2 * n + h + 1)
                nc.vector.tensor_tensor(wu_lo[:, s, :], wu_raw[:, s, :], wu_hi[:, s, :].bitcast(f32),
                                        ALU.subtract).then_inc(wu_lo_done, 1)

            def split_wd(n):
                for t in range(FT):
                    dve.wait_ge(wd_hi_done, FT * n + t + 1)
                    nc.vector.tensor_tensor(wd_lo[:, t, :], wd_raw[:, t, :], wd_hi[:, t, :].bitcast(f32),
                                            ALU.subtract).then_inc(wd_lo_done, 1)

            def split_a(n, slot, t):
                dve.wait_ge(a_hi_done, FT * n + t + 1)
                dve.wait_ge(square_done, FT * n + t + 1)
                nc.vector.tensor_tensor(a_lo[:, slot, t, :], square[:, t, :], a_hi[:, slot, t, :].bitcast(f32),
                                        ALU.subtract).then_inc(a_lo_done, 1)

            def add_down(outs, o, base=acc):
                j, c = o // NH, slice((o % NH) * HALF, (o % NH + 1) * HALF)
                dve.wait_ge(ring_full, outs + o + 1)
                nc.vector.tensor_tensor(acc[:, j, c], ring_ps[:, o % RING, :], base[:, j, c],
                                        ALU.add).then_inc(ring_read, 1)

            def add_pooled(m, w, outs):
                for j in range(TT):
                    c = ds(w * WC, WC)
                    dve.wait_ge(ring_full, outs + j + 1)
                    nc.vector.tensor_tensor(x1[:, j, c], ring_ps[:, j, 0:WC], xr[:, j, c],
                                            ALU.add).then_inc(ring_read, 1)

            def subtract_own(m, w):
                dve.wait_ge(summed, SUM_STEPS[WINDOWS] * m + SUM_STEPS[w + 1])
                s = sums[w % 2][:, :, HALO:HALO + GT]
                nc.vector.scalar_tensor_tensor(s, s, 0.5 ** (w + 1), ht[:, :, HALO:HALO + GT],
                                               ALU.mult, ALU.subtract).then_inc(diff_done, 1)

            def split_pooled(m, w):
                dve.wait_ge(dt_hi_done, WINDOWS * m + w + 1)
                nc.vector.tensor_tensor(dt_lo[:, :, :], sums[w % 2][:, :, HALO:HALO + GT],
                                        dt_hi[:, :, :].bitcast(f32), ALU.subtract).then_inc(dt_lo_done, 1)

            def split_h2(m, d):
                dve.wait_ge(h2_hi_done, DT * m + d + 1)
                nc.vector.scalar_tensor_tensor(h2_lo[:, d, :], mix_ps[:, d % 2, :], g_mlp_c[:, d:d + 1],
                                               h2_hi[:, d, :].bitcast(f32),
                                               ALU.mult, ALU.subtract).then_inc(h2_lo_done, 1)

            def finish(g, j):
                dve.wait_ge(rs_f_done, TT * g + j + 1)
                nc.vector.scalar_tensor_tensor(acc[:, j, :], acc[:, j, :], rs_f[:, j:j + 1], g_fin_b[:, :],
                                               ALU.mult, ALU.mult).then_inc(final_done, 1)

            nc.vector.memset(power[:, :], -0.5).then_inc(const_set, 1)
            nc.vector.memset(eps[:, :], EPS).then_inc(const_set, 1)
            nc.vector.memset(ms_x[:, :], 1.0).then_inc(const_set, 1)
            nc.vector.memset(xw[:, TT, :], 0.0).then_inc(const_set, 1)
            dve.wait_ge(acc_moved, ACC_LOADS)
            dve.wait_ge(g_mix_in, 16)
            for q in range(WINDOWS * CT):
                nc.vector.scalar_tensor_tensor(pw_raw[:, q, :], pw_raw[:, q, :], g_mix_c[:, q:q + 1],
                                               scale_b[:, (q // CT) * WC:(q // CT + 1) * WC],
                                               ALU.mult, ALU.mult).then_inc(pool_scaled, 1)
            for w in range(WINDOWS):
                if w > 0:
                    dve.wait_ge(dt_lo_done, w)
                window_sums(nc.vector, dve, 0, w)
                subtract_own(0, w)
                if w == 0:
                    for q in range(2):
                        s = slice(4 * q, 4 * q + 4)
                        dve.wait_ge(pool_hi, q + 1)
                        nc.vector.tensor_tensor(pw_lo[:, s, :], pw_raw[:, s, :], pw_hi[:, s, :].bitcast(f32),
                                                ALU.subtract).then_inc(pool_lo, 1)
                split_pooled(0, w)
                if w > 0:
                    add_pooled(0, w - 1, (w - 1) * TT)
            add_pooled(0, WINDOWS - 1, FIRST_OUTS - TT)
            dve.wait_ge(gain_in, 48)
            split_wu(0, 0)
            split_wu(0, 1)
            for d in range(DT):
                split_h2(0, d)
            split_wu(1, 0)
            split_wu(1, 1)

            def step(n, slot, outs, after={}, first_of=None):
                split_wd(n - 1)
                for t in range(FT):
                    split_a(n - 1, slot, t)
                if first_of is not None:
                    dve.wait_ge(acc_moved, ACC_LOADS + 16 * TT * first_of)
                for o in range(OUTS):
                    add_down(outs, o, acc if first_of is None else x1)
                    if o < 2:
                        split_wu(n + 1, o)
                    for work in after.get(o, []):
                        work()

            def pair(n, outs, first_of=None):
                step(n, 0, outs, first_of=first_of)
                step(n + 1, 1, outs + OUTS)

            def mix_pair(g, w):
                n = CHUNKS * g + 2 * w + 1
                outs = ring_base(g) + w * MIX_PAIR_OUTS
                step(n, 0, outs, first_of=g if w == 0 else None)
                step(n + 1, 1, outs + OUTS, {2: [lambda: subtract_own(g + 1, w)],
                                             4: [lambda: split_pooled(g + 1, w)]})
                add_pooled(g + 1, w, outs + PAIR_OUTS)

            with dve.Fori(0, GROUPS - 1) as g:
                n0 = CHUNKS * g
                outs = ring_base(g)
                for w in range(MIX_PAIRS):
                    mix_pair(g, w)
                with dve.Fori(MIX_PAIRS, PAIRS - 1) as i:
                    pair(n0 + 2 * i + 1, outs + WINDOWS * TT + i * PAIR_OUTS)
                n = n0 + CHUNKS - 1
                last = outs + GROUP_OUTS - PAIR_OUTS
                split_wd(n - 1)
                split_a(n - 1, 0, 0)
                split_a(n - 1, 0, 1)
                split_h2(g + 1, 0)
                split_h2(g + 1, 1)
                for o in range(OUTS):
                    add_down(last, o)
                    if o < 2:
                        split_wu(n + 1, o)
                    if o + 2 < DT:
                        split_h2(g + 1, o + 2)
                step(n + 1, 1, last + OUTS,
                     {NH * (j + 2) - 1: [lambda j=j: finish(g, j)] for j in range(TT - 1)})
                finish(g, TT - 1)
            g = GROUPS - 1
            n0 = CHUNKS * g
            pair(n0 + 1, LAST_BASE, first_of=g)
            with dve.Fori(1, PAIRS - 1) as i:
                pair(n0 + 2 * i + 1, LAST_BASE + i * PAIR_OUTS)
            n = n0 + CHUNKS - 1
            last = LAST_BASE + (PAIRS - 1) * PAIR_OUTS
            split_wd(n - 1)
            split_a(n - 1, 0, 0)
            split_a(n - 1, 0, 1)
            for o in range(OUTS):
                add_down(last, o)
                if 2 <= o < 2 + FT:
                    t = o - 2
                    split_a(n, 1, t)
                    dve.wait_ge(wd_hi_done, FT * n + t + 1)
                    nc.vector.tensor_tensor(wd_last_lo[:, NH * t:NH * (t + 1), :],
                                            wd_raw[:, t, :].rearrange("p (h e) -> p h e", h=NH),
                                            wd_last_hi[:, NH * t:NH * (t + 1), :].bitcast(f32),
                                            ALU.subtract).then_inc(wd_lo_done, 1)
            for o in range(OUTS):
                add_down(last + OUTS, o)
                if o % NH == NH - 1 and o >= 2 * NH - 1:
                    finish(g, o // NH - 1)
            finish(g, TT - 1)

        @block.gpsimd
        def _(pool):
            def squares(n, first=False):
                for t in range(FT):
                    pool.wait_ge(relu_done, FT * n + t + 1)
                    if not first:
                        pool.wait_ge(a_lo_done, FT * (n - 1) + t + 1)
                    nc.gpsimd.tensor_tensor(square[:, t, :], relu[:, t, :], relu[:, t, :],
                                            ALU.mult).then_inc(square_done, 1)

            def rms(ms, me, rs, width, me_sem, count, rs_sem):
                nc.gpsimd.tensor_tensor(me, ms, eps[:, 0:width], ALU.add).then_inc(me_sem, 1)
                pool.wait_ge(me_sem, count)
                nc.gpsimd.tensor_tensor(rs, me, power[:, 0:width], ALU.pow).then_inc(rs_sem, 1)

            def row_rms(m):
                pool.wait_ge(ms_x_done, NORMS * (m + 1))
                rms(ms_x[:, :], me_x[:, :], rs_x[:, :], NORMS, me_x_done, m + 1, rs_x_done)

            def mixed_rms(m):
                pool.wait_ge(ms_m_done, TT * (m + 1))
                rms(ms_m[:, :], me_m[:, :], rs_m[:, :], TT, me_m_done, m + 1, rs_m_done)

            def final_rms(g):
                for j in range(TT):
                    c = slice(j, j + 1)
                    pool.wait_ge(ms_f_done, TT * g + j + 1)
                    rms(ms_f[:, c], me_f[:, c], rs_f[:, c], 1, me_f_done, TT * g + j + 1, rs_f_done)

            pool.wait_ge(const_set, 4)
            row_rms(0)
            mixed_rms(0)
            squares(0, first=True)
            with pool.Fori(0, GROUPS - 1) as g:
                n0 = CHUNKS * g
                row_rms(g + 1)
                for w in range(MIX_PAIRS):
                    squares(n0 + 2 * w + 1)
                    window_sums(nc.gpsimd, pool, g + 1, w)
                    squares(n0 + 2 * w + 2)
                squares(n0 + 2 * MIX_PAIRS + 1)
                mixed_rms(g + 1)
                with pool.Fori(2 * MIX_PAIRS + 1, CHUNKS) as i:
                    squares(n0 + i + 1)
                final_rms(g)
            n0 = CHUNKS * (GROUPS - 1)
            with pool.Fori(1, CHUNKS) as i:
                squares(n0 + i)
            final_rms(GROUPS - 1)

        @block.tensor
        def _(pe):
            def up_tile(n, t, each=lambda d: None):
                c = slice(t * P, (t + 1) * P)
                for d in range(DT):
                    if t == 0 and d % (DT // 2) == 0:
                        pe.wait_ge(wu_lo_done, 2 * n + d // (DT // 2) + 1)
                    each(d)
                    o = up_ps[:, t, :]
                    nc.tensor.matmul(o, wu_hi[:, d, c], h2_hi[:, d, :], start=(d == 0), stop=False)
                    nc.tensor.matmul(o, wu_hi[:, d, c], h2_lo[:, d, :], start=False, stop=False)
                    last = nc.tensor.matmul(o, wu_lo[:, d, c], h2_hi[:, d, :], start=False, stop=(d == DT - 1))
                last.then_inc(up_done, 1)

            def up(n):
                for t in range(FT):
                    pe.wait_ge(relu_done, FT * (n - 1) + t + 1)
                    up_tile(n, t)

            def down_out(slot, outs, o, final=False):
                j, h = o // NH, o % NH
                r = slice(j * P, (j + 1) * P)
                c = slice(h * HALF, (h + 1) * HALF)
                pe.wait_ge(ring_read, outs + o + 1 - RING)
                dst = ring_ps[:, o % RING, :]
                for t in range(FT):
                    hi, lo = wd_hi[:, t, c], wd_lo[:, t, c]
                    if final:
                        hi, lo = wd_last_hi[:, NH * t + h, :], wd_last_lo[:, NH * t + h, :]
                    nc.tensor.matmul(dst, a_hi[:, slot, t, r], hi, start=(t == 0), stop=False)
                    nc.tensor.matmul(dst, a_hi[:, slot, t, r], lo, start=False, stop=False)
                    last = nc.tensor.matmul(dst, a_lo[:, slot, t, r], hi, start=False, stop=(t == FT - 1))
                last.then_inc(ring_full, 1)

            def down_ready(n):
                pe.wait_ge(wd_lo_done, FT * (n + 1))
                pe.wait_ge(a_lo_done, FT * (n + 1))

            def down(n, slot, outs, final=False, after={}):
                down_ready(n)
                for o in range(OUTS):
                    down_out(slot, outs, o, final)
                    for work in after.get(o, []):
                        work()

            def turn_window(m, w):
                v = WINDOWS * m + w
                pe.wait_ge(xw_done, NORMS * (v + 1))
                for c in range(CT):
                    for j in range(TT):
                        last = nc.tensor.transpose(mix_ps[:, c, j * P:(j + 1) * P],
                                                   xw[:, j, c * P:(c + 1) * P], ident[:, :])
                    last.then_inc(x_turned, 1)

            def turn_halos(m, w):
                pe.wait_ge(ht_done, TURNS * (WINDOWS * m + w) + 1)
                for c in range(CT):
                    last = nc.tensor.transpose(mix_ps[:, 0, c * P:(c + 1) * P],
                                               xw[:, TT, c * P:(c + 1) * P], ident[:, :])
                last.then_inc(x_turned, 1)

            def pool_out(m, w, outs, first=False):
                pe.wait_ge(dt_lo_done, WINDOWS * m + w + 1)
                for j in range(TT):
                    r = slice(j * P, (j + 1) * P)
                    if not first:
                        pe.wait_ge(ring_read, outs + j + 1 - RING)
                    dst = ring_ps[:, j, 0:WC]
                    for c in range(CT):
                        q = w * CT + c
                        nc.tensor.matmul(dst, dt_hi[:, c, r], pw_hi[:, q, :], start=(c == 0), stop=False)
                        nc.tensor.matmul(dst, dt_hi[:, c, r], pw_lo[:, q, :], start=False, stop=False)
                        last = nc.tensor.matmul(dst, dt_lo[:, c, r], pw_hi[:, q, :], start=False, stop=(c == CT - 1))
                    last.then_inc(ring_full, 1)

            def transpose(m, d):
                if d < 2:
                    pe.wait_ge(ht_done, TURNS * WINDOWS * (m + 1))
                else:
                    pe.wait_ge(h2_lo_done, DT * m + d - 1)
                for j in range(TT):
                    last = nc.tensor.transpose(mix_ps[:, d % 2, j * P:(j + 1) * P],
                                               xr[:, j, d * P:(d + 1) * P], ident[:, :])
                last.then_inc(transposed, 1)

            pe.wait_ge(gain_in, 48)
            for w in range(WINDOWS):
                if w > 0:
                    pe.wait_ge(ht_done, TURNS * w)
                turn_window(0, w)
                turn_halos(0, w)
                if w == 1:
                    pe.wait_ge(pool_lo, 2)
                if w > 0:
                    pool_out(0, w - 1, (w - 1) * TT, first=(w == 1))
            pool_out(0, WINDOWS - 1, FIRST_OUTS - TT)
            pe.wait_ge(x1n_done, TT)
            transpose(0, 0)
            transpose(0, 1)

            def next_tile(d):
                if d + 2 < DT:
                    transpose(0, d + 2)
                pe.wait_ge(h2_lo_done, d + 1)

            up_tile(0, 0, next_tile)
            up_tile(0, 1)

            with pe.Fori(0, GROUPS - 1) as g:
                n0 = CHUNKS * g
                outs = ring_base(g)
                with pe.Fori(0, MIX_PAIRS) as w:
                    n = n0 + 2 * w + 1
                    outs_w = outs + w * MIX_PAIR_OUTS
                    up(n)
                    pe.wait_ge(h2_lo_done, DT * (g + 1))
                    pe.wait_ge(ht_done, TURNS * (WINDOWS * (g + 1) + w))
                    down(n - 1, 0, outs_w, after={5: [lambda: turn_window(g + 1, w)],
                                                  7: [lambda: turn_halos(g + 1, w)]})
                    up(n + 1)
                    down(n, 1, outs_w + OUTS)
                    pool_out(g + 1, w, outs_w + PAIR_OUTS)
                with pe.Fori(0, PAIRS - 1 - MIX_PAIRS) as i:
                    n = n0 + 2 * (i + MIX_PAIRS) + 1
                    outs_i = outs + MIX_END + i * PAIR_OUTS
                    up(n)
                    down(n - 1, 0, outs_i)
                    up(n + 1)
                    down(n, 1, outs_i + OUTS)
                n = n0 + CHUNKS - 1
                last = outs + GROUP_OUTS - PAIR_OUTS
                up(n)
                down_ready(n - 1)
                pe.wait_ge(x1n_done, TT * (g + 2))
                transpose(g + 1, 0)
                transpose(g + 1, 1)
                for o in range(OUTS):
                    down_out(0, last, o)
                    if o + 2 < DT:
                        transpose(g + 1, o + 2)
                pe.wait_ge(h2_lo_done, DT * (g + 2))
                up(n + 1)
                down(n, 1, last + OUTS)
            n0 = CHUNKS * (GROUPS - 1)
            with pe.Fori(0, PAIRS - 1) as i:
                n = n0 + 2 * i + 1
                outs_i = LAST_BASE + i * PAIR_OUTS
                up(n)
                down(n - 1, 0, outs_i)
                up(n + 1)
                down(n, 1, outs_i + OUTS)
            n = n0 + CHUNKS - 1
            last = LAST_BASE + (PAIRS - 1) * PAIR_OUTS
            up(n)
            down(n - 1, 0, last)
            down(n, 1, last + OUTS, final=True)


def end_scales():
    import numpy as np

    scale = np.ones((GROUPS, WINDOWS, 2, HALO), np.float32)
    for w in range(WINDOWS):
        half = 2 ** w
        for t in range(HALO):
            for g in (0, GROUPS - 1):
                scale[g, w, 0, t] = 2 * half / (min(t, half) + half)
            for g in (GROUPS - 2, GROUPS - 1):
                scale[g, w, 1, t] = 2 * half / (half + min(HALO - t, half))
    scale = np.broadcast_to(scale[:, None, :, None], (GROUPS, P, WINDOWS, CT, 2, HALO))
    return np.ascontiguousarray(scale)


def kernel(x_prompt, x_sample, norm_mix_g, norm_mlp_g, w_up, w_down, final_norm_g, pool_w, pool_scale, **unused):
    import concourse.bacc as bacc
    import numpy as np
    from concourse.bass_utils import run_bass_kernel_spmd

    seqs = [np.asarray(x_prompt)[0], np.asarray(x_sample)[0]]
    halos = []
    for seq in seqs:
        edge = np.zeros((HALO, D), np.float32)
        rows = np.concatenate([edge, seq, edge])
        for at in range(0, len(seq), GT):
            halos.append(np.concatenate([rows[at:at + HALO], rows[at + HALO + GT:at + HT]]))
    arrays = {
        "x": np.concatenate(seqs).reshape(GROUPS, GT, D),
        "halos": np.stack(halos),
        "w_up": np.ascontiguousarray(np.asarray(w_up)[0]),
        "w_down": np.ascontiguousarray(np.asarray(w_down)[0]),
        "pool_w": np.ascontiguousarray(np.asarray(pool_w)[0]),
        "pool_scale": np.ascontiguousarray(np.asarray(pool_scale)[0]),
        "g_mix": np.ascontiguousarray(np.asarray(norm_mix_g)[0].reshape(DT, P).T),
        "g_mlp": np.ascontiguousarray(np.asarray(norm_mlp_g)[0].reshape(DT, P).T),
        "g_fin": np.ascontiguousarray(np.asarray(final_norm_g)),
        "ends": end_scales(),
        "ident_in": np.eye(P, dtype=np.float32),
    }
    nc = bacc.Bacc("TRN2", target_bir_lowering=False, num_devices=1)
    args = [nc.dram_tensor(name, a.shape, mybir.dt.float32, kind="ExternalInput").ap() for name, a in arrays.items()]
    out = nc.dram_tensor("out", (GROUPS, GT, D), mybir.dt.float32, kind="ExternalOutput").ap()
    build(nc, *args, out)
    r = run_bass_kernel_spmd(nc, [arrays], core_ids=[0])
    y = r.results[0]["out"].reshape(1, GROUPS * GT, D)
    n = len(seqs[0])
    return y[:, :n], y[:, n:]
```

```python
from contextlib import ExitStack

import concourse.bass as bass
from concourse import mybir
from concourse.alu_op_type import AluOpType as ALU

P = 128
D = 1024
F = 4096
GT = 512
GROUPS = 5
EPS = 1e-6
WINDOWS = 4
WC = D // WINDOWS
CT = WC // P
HALO = 8
HT = GT + 2 * HALO
NORMS = GT // P + 1
FC = 256
CHUNKS = F // FC
FT = FC // P
DT = D // P
TT = GT // P
HALF = 512
NH = D // HALF
OUTS = TT * NH
RING = 4
MIX_PAIRS = WINDOWS
PAIRS = CHUNKS // 2
PAIR_OUTS = 2 * OUTS
MIX_PAIR_OUTS = PAIR_OUTS + TT
GROUP_OUTS = PAIRS * PAIR_OUTS + WINDOWS * TT
ACC_LOADS = 16
FIRST_OUTS = WINDOWS * TT
TURNS = CT + 1
INNER = P - 2 * HALO
CUTS = [P - HALO + i * INNER for i in range(TT)]
OUT_AT = [0] + CUTS
OUT_N = [b - a for a, b in zip(OUT_AT, CUTS + [GT])]
ROW_AT = [0] + [c - HALO for c in CUTS]
ROW_N = [min(P, GT + HALO - at) for at in ROW_AT]
TILES = len(OUT_AT)
BAND = OUT_N[0]
TILE_ORDER = (0, 1, 4, 2, 3)
ACT_TILES = (0, 1, 4)
DVE_TILES = (2, 3)
LAST = GROUPS - 1
SLOTS = D // WC
WARM_UP = (20, 18)
FIRST = 0
SUM_STEPS = [sum(v + 2 for v in range(w)) for w in range(WINDOWS + 1)]


def build(nc, x, halos, w_up, w_down, pool_w, pool_scale, g_mix, g_mlp, g_fin, ends, bands, ident_in,
          out):
    f32 = mybir.dt.float32
    f32r = mybir.dt.float32r
    ACT = mybir.ActivationFunctionType
    ds = bass.ds

    pool_w_v = pool_w.rearrange("g (t p) e -> p (g t) e", p=P)

    ctx = ExitStack()
    with ctx:
        def sb(name, shape, dt=f32):
            return ctx.enter_context(nc.sbuf_tensor(name, shape, dt))

        def pb(name, shape):
            return ctx.enter_context(nc.psum_tensor(name, shape, f32))

        def sem(name):
            return ctx.enter_context(nc.semaphore(name))

        with ExitStack() as rooms:
            def room(name, shape):
                return rooms.enter_context(nc.sbuf_tensor(name, shape, f32))

            first_x = room("first_x", [P, TILES, D])
            band = room("band", [P, 2, WINDOWS, BAND])
            band_x = room("band_x", [P, TILES, WINDOWS, BAND])

        h2_hi = sb("h2_hi", [P, DT, GT], f32r)
        h2_lo = sb("h2_lo", [P, DT, GT], f32r)
        wd_hi = sb("wd_hi", [P, FT, D], f32r)
        wd_lo = sb("wd_lo", [P, FT, D], f32r)
        wu_raw = sb("wu_raw", [P, FT, DT, P])
        wu_hi = sb("wu_hi", [P, FT, DT, P], f32r)
        wu_lo = sb("wu_lo", [P, FT, DT, P], f32r)
        wd_raw = sb("wd_raw", [P, FT, D])
        relu = sb("relu", [P, FT, GT])
        square = sb("square", [P, FT, GT])
        a_hi = sb("a_hi", [P, 2, FT, GT], f32r)
        a_lo = sb("a_lo", [P, 2, FT, GT], f32r)
        wd_last_hi = h2_hi[:, 0:FT * NH, :]
        wd_last_lo = h2_lo[:, 0:FT * NH, :]
        acc = sb("acc", [P, TT, D])
        xr = sb("xr", [P, TT, D])
        xh = sb("xh", [2 * HALO, D])
        xw = sb("xw", [P, NORMS, WC])
        ht = sb("ht", [P, CT, HT])
        sums = [sb(f"sums{i}", [P, CT, HT]) for i in range(2)]
        end_scale = sb("end_scale", [P, WINDOWS, CT, 2, HALO])
        dt_hi = sb("dt_hi", [P, CT, GT], f32r)
        dt_lo = sb("dt_lo", [P, CT, GT], f32r)
        junk = dt_hi[:, :, :].rearrange("p c t -> p (c t)")
        x1 = sb("x1", [P, TT, D])
        pw_hi = sb("pw_hi", [P, WINDOWS * CT, WC], f32r)
        pw_lo = sb("pw_lo", [P, WINDOWS * CT, WC], f32r)
        g_fin_b = sb("g_fin_b", [P, D])
        g_mix_c = sb("g_mix_c", [P, DT])
        g_mlp_c = sb("g_mlp_c", [P, DT])
        ident = sb("ident", [P, P])
        power = sb("power", [P, NORMS])
        eps = sb("eps", [P, NORMS])
        warm = sb("warm", [P, 1])
        warm_square = sb("warm_square", [P, 1])
        ms_x = sb("ms_x", [P, NORMS])
        me_x = sb("me_x", [P, NORMS])
        rs_x = sb("rs_x", [P, NORMS])
        ms_m = sb("ms_m", [P, TT])
        ms_part = sb("ms_part", [P, WINDOWS, TT])
        me_m = sb("me_m", [P, TT])
        rs_m = sb("rs_m", [P, TT])
        ms_f = sb("ms_f", [P, TT])
        ms_end = sb("ms_end", [P, 1])
        me_end = sb("me_end", [P, 1])
        me_f = sb("me_f", [P, TT])
        rs_f = sb("rs_f", [P, TT])
        pw_raw = acc[:, 0:2, :].rearrange("p a (b e) -> p (a b) e", e=WC)
        scale_b = acc[:, 2, :]

        row_squares = [x1[:, i, :] for i in range(TT)] + [junk]
        first_squares = square[:, :, :].rearrange("p c t -> p (c t)")
        wd_room = [wd_lo[:, t, :].rearrange("p (c t) -> p c t", c=CT) for t in range(FT)]
        first_dt = [(dt_hi[:, :, :], dt_lo[:, :, :]), wd_room,
                    (a_hi[:, 0, :, :], a_hi[:, 1, :, :]), (a_lo[:, 0, :, :], a_lo[:, 1, :, :])]

        up_ps = pb("up_ps", [P, FT, HALF])
        ring_ps = pb("ring_ps", [P, RING, HALF])
        mix_ps = pb("mix_ps", [P, 2, HALF])
        first_banks = [mix_ps[:, :, :], up_ps[:, :, :], ring_ps[:, 0:2, :], ring_ps[:, 2:4, :]]

        def first_out_bank(w, j):
            if w == 0:
                return (mix_ps if j < 2 else up_ps)[:, j % 2, :]
            return ring_ps[:, j, :]

        def h2_bank(m, d):
            if m is FIRST and d % 6 > 1:
                return ring_ps[:, d % 6 - 2, :]
            return mix_ps[:, d % (6 if m is FIRST else 2), :]

        acc_moved = sem("acc_moved")
        g_mix_in = sem("g_mix_in")
        gain_in = sem("gain_in")
        ident_loaded = sem("ident_loaded")
        const_set = sem("const_set")
        pool_scaled = sem("pool_scaled")
        pool_hi = sem("pool_hi")
        pool_lo = sem("pool_lo")
        wu_in = [sem(f"wu_in{t}") for t in range(FT)]
        wu_hi_done = sem("wu_hi_done")
        wu_lo_done = sem("wu_lo_done")
        wd_in = sem("wd_in")
        wd_hi_done = sem("wd_hi_done")
        wd_lo_done = sem("wd_lo_done")
        up_done = sem("up_done")
        relu_done = sem("relu_done")
        square_done = sem("square_done")
        a_hi_done = sem("a_hi_done")
        a_lo_done = sem("a_lo_done")
        ring_full = sem("ring_full")
        ring_read = sem("ring_read")
        xr_in = [sem(f"xr_in{j}") for j in range(TT)]
        halo_in = sem("halo_in")
        ends_in = sem("ends_in")
        first_in = [sem(f"first_in{i}") for i in range(TILES)]
        first_ms_done = [sem(f"first_ms_done{i}") for i in range(TILES)]
        first_me_done = sem("first_me_done")
        first_rs_done = sem("first_rs_done")
        band_in = [sem(f"band_in{i}") for i in range(2)]
        band_scaled = [sem(f"band_scaled{i}") for i in range(TILES)]
        pw_in = [sem(f"pw_in{w}") for w in range(WINDOWS)]
        banded = sem("banded")
        first_hi_done = sem("first_hi_done")
        first_lo_done = sem("first_lo_done")
        first_rs_m_done = sem("first_rs_m_done")
        first_x1n = [sem(f"first_x1n{h}") for h in range(NH)]
        ms_x_done = sem("ms_x_done")
        me_x_done = sem("me_x_done")
        rs_x_done = sem("rs_x_done")
        xw_done = sem("xw_done")
        x_turned = sem("x_turned")
        ht_done = sem("ht_done")
        summed = sem("summed")
        diff_done = sem("diff_done")
        dt_hi_done = sem("dt_hi_done")
        dt_lo_done = sem("dt_lo_done")
        ms_part_done = sem("ms_part_done")
        ms_m_done = sem("ms_m_done")
        me_m_done = sem("me_m_done")
        rs_m_done = sem("rs_m_done")
        x1n_done = sem("x1n_done")
        transposed = sem("transposed")
        h2_hi_done = sem("h2_hi_done")
        h2_lo_done = sem("h2_lo_done")
        ms_f_done = sem("ms_f_done")
        me_f_done = sem("me_f_done")
        rs_f_done = sem("rs_f_done")
        final_done = sem("final_done")

        block = ctx.enter_context(nc.Block())

        def ring_base(g):
            return FIRST_OUTS + g * GROUP_OUTS

        LAST_BASE = ring_base(GROUPS - 1)
        MIX_END = MIX_PAIRS * MIX_PAIR_OUTS

        def window_sums(engine, eng, w, ht, room, done_sem, done):
            src = ht
            for level in range(w + 1):
                shift = 2 ** level
                last = level == w
                first = HALO - 2 ** w
                n = GT + 2 ** (w + 1) - 2 * shift
                dst, to = room[level % 2], (2 ** w if last else 0)
                engine.tensor_tensor(dst[:, :, first + to:first + to + n], src[:, :, first:first + n],
                                     src[:, :, first + shift:first + shift + n], ALU.add).then_inc(done_sem, 1)
                done = done + 1
                eng.wait_ge(done_sem, done)
                src = dst
            ends_of = src[:, :, HALO:HALO + GT].rearrange("p c (a b) -> p c a b", b=HALO)
            both = ends_of[:, :, 0:GT // HALO:GT // HALO - 1, :]
            engine.tensor_tensor(both, both, end_scale[:, w, :, :, :], ALU.mult).then_inc(done_sem, 1)

        @block.sync
        def _(sp):
            def load_wu(k, t):
                sp.dma_start(wu_raw[:, t, :, :], w_up[k, t]).then_inc(wu_in[t], 16)

            def next_wu(n, k):
                for t in range(FT):
                    sp.wait_ge(wu_lo_done, FT * (n - 1) + t + 1)
                    load_wu(k, t)

            def load_wd(k):
                sp.dma_start(wd_raw[:, :, :], w_down[k]).then_inc(wd_in, 16)

            def step(n, k, k_next):
                next_wu(n + 1, k_next)
                sp.wait_ge(wd_lo_done, FT * n)
                load_wd(k)

            def load_rows(m):
                for j in range(TT):
                    sp.dma_start(xr[:, j, :], x[m, j * P:(j + 1) * P, :]).then_inc(xr_in[j], 16)

            def load_halos(m):
                sp.dma_start(xh[:, :], halos[m]).then_inc(halo_in, 16)

            def load_ends(m):
                sp.dma_start(end_scale[:, :, :, :, :], ends[m]).then_inc(ends_in, 16)

            def store(g):
                for j in range(TT if g is not LAST else TT - 1):
                    sp.wait_ge(final_done, TT * g + j + 1)
                    sp.dma_start(out[g, j * P:(j + 1) * P, :], acc[:, j, :]).then_inc(acc_moved, 16)
                if g is LAST:
                    j = TT - 1
                    for h in range(NH):
                        c = slice(h * HALF, (h + 1) * HALF)
                        sp.wait_ge(final_done, TT * g + j + 1 + h)
                        sp.dma_start(out[g, j * P:(j + 1) * P, c], acc[:, j, c]).then_inc(acc_moved, 16)

            def prefetch_rows(m):
                sp.wait_ge(transposed, DT * m)
                load_rows(m)
                sp.wait_ge(xw_done, NORMS * WINDOWS * (m - 1))
                load_halos(m)
                sp.wait_ge(summed, SUM_STEPS[WINDOWS] * (m - 1))
                load_ends(m)

            x_rows = x.rearrange("g t d -> (g t) d")
            sp.dma_start(ident[:, :], ident_in).then_inc(ident_loaded, 16)
            for i in TILE_ORDER:
                sp.dma_start(first_x[0:ROW_N[i], i, :],
                             x_rows[ROW_AT[i]:ROW_AT[i] + ROW_N[i], :]).then_inc(first_in[i], 16)
                if i < 2:
                    sp.dma_start(band[:, i, :, :], bands[:, i, :, :]).then_inc(band_in[i], 16)
            sp.dma_start(g_mix_c[:, :], g_mix).then_inc(g_mix_in, 16)
            sp.dma_start(scale_b, pool_scale.partition_broadcast(P)).then_inc(acc_moved, 16)
            for w in range(WINDOWS):
                part = slice(w * CT, (w + 1) * CT)
                sp.dma_start(pw_raw[:, part, :], pool_w_v[:, part, :]).then_inc(pw_in[w], 16)
            load_rows(0)
            sp.dma_start(g_mlp_c[:, :], g_mlp).then_inc(gain_in, 16)
            sp.dma_start(g_fin_b[:, :], g_fin.partition_broadcast(P)).then_inc(gain_in, 16)
            for t in range(FT):
                load_wu(0, t)
            load_wd(0)
            load_ends(1)
            load_halos(1)
            next_wu(1, 1)
            sp.wait_ge(transposed, DT)
            load_rows(1)
            next_wu(2, 2)

            def group(g, mixer, prefetch):
                n0 = CHUNKS * g
                sp.wait_ge(wd_lo_done, 2 * (n0 + 1))
                load_wd(1)
                with sp.Fori(2, CHUNKS - 1) as k:
                    step(n0 + k, k, k + 1)
                if mixer:
                    step(n0 + CHUNKS - 1, CHUNKS - 1, 0)
                    step(n0 + CHUNKS, 0, 1)
                else:
                    sp.wait_ge(wd_lo_done, 2 * (n0 + CHUNKS - 1))
                    load_wd(CHUNKS - 1)
                if prefetch:
                    prefetch_rows(g + 2)
                if mixer:
                    next_wu(n0 + CHUNKS + 2, 2)
                store(g)

            with sp.Fori(0, GROUPS - 2) as g:
                group(g, True, True)
            group(GROUPS - 2, True, False)
            group(LAST, False, False)
            sp.wait_ge(acc_moved, ACC_LOADS + 16 * (TT * GROUPS + NH - 1))

        @block.scalar
        def _(act):
            def split_wu(n, t, first=False):
                act.wait_ge(wu_in[t], 16 * (n + 1))
                if not first:
                    act.wait_ge(up_done, FT * (n - 1) + t + 1)
                nc.scalar.copy(wu_hi[:, t, :, :], wu_raw[:, t, :, :]).then_inc(wu_hi_done, 1)

            def split_wd(n, outs_before):
                for t in range(FT):
                    act.wait_ge(wd_in, 16 * (n + 1))
                    act.wait_ge(ring_full, outs_before)
                    nc.scalar.copy(wd_hi[:, t, :], wd_raw[:, t, :]).then_inc(wd_hi_done, 1)

            def activate(n, slot, t, first=False):
                act.wait_ge(up_done, FT * n + t + 1)
                if not first:
                    act.wait_ge(square_done, FT * (n - 1) + t + 1)
                nc.scalar.activation(relu[:, t, :], up_ps[:, t, :], ACT.Relu).then_inc(relu_done, 1)
                act.wait_ge(relu_done, FT * n + t + 1)
                nc.scalar.activation(a_hi[:, slot, t, :], relu[:, t, :], ACT.Square).then_inc(a_hi_done, 1)

            def follow_up(n, slot, first=False):
                for t in range(FT):
                    activate(n, slot, t, first)
                    split_wu(n + 1, t)

            def mean_square(src, dst, rows=P, squares=junk):
                return nc.scalar.activation(squares[0:rows, :], src, ACT.Square, scale=D ** -0.5, accum_out=dst)

            def row_stats(m):
                for j in range(NORMS):
                    act.wait_ge(*((xr_in[j], 16 * (m + 1)) if j < TT else (halo_in, 16 * m)))
                    if j > 0:
                        act.wait_ge(ms_x_done, NORMS * (m - 1) + j)
                    rows, src = (P, xr[:, j, :]) if j < TT else (2 * HALO, xh[:, :])
                    mean_square(src, ms_x[0:rows, j:j + 1], rows).then_inc(ms_x_done, 1)

            def norm_rows(m, w):
                act.wait_ge(rs_x_done, m)
                for j in range(NORMS):
                    rows, src = (P, xr[:, j, ds(w * WC, WC)]) if j < TT else (2 * HALO, xh[:, ds(w * WC, WC)])
                    nc.scalar.activation(xw[0:rows, j, :], src, ACT.Copy,
                                         scale=rs_x[0:rows, j:j + 1]).then_inc(xw_done, 1)

            def keep_turned(m, w):
                v = WINDOWS * (m - 1) + w
                for c in range(CT):
                    act.wait_ge(x_turned, TURNS * v + c + 1)
                    nc.scalar.copy(ht[:, c, HALO:HALO + GT], mix_ps[:, c, :]).then_inc(ht_done, 1)
                act.wait_ge(x_turned, TURNS * v + TURNS)
                both = ht[:, :, :].rearrange("p c (a b) -> p c a b", b=HALO)[:, :, 0:HT // HALO:HT // HALO - 1, :]
                src = mix_ps[:, 0, 0:CT * P].rearrange("p (c a b) -> p c a b", c=CT, b=HALO)[:, :, 0:2, :]
                nc.scalar.copy(both, src).then_inc(ht_done, 1)

            def split_pooled(m, w):
                act.wait_ge(diff_done, WINDOWS * (m - 1) + w + 1)
                nc.scalar.copy(dt_hi[:, :, :], sums[w % 2][:, :, HALO:HALO + GT]).then_inc(dt_hi_done, 1)

            def mixed_stats(m, outs):
                act.wait_ge(ring_read, outs)
                for j in range(TT):
                    if j > 0:
                        act.wait_ge(ms_m_done, TT * (m - 1) + j)
                    mean_square(x1[:, j, :], ms_m[:, j:j + 1]).then_inc(ms_m_done, 1)

            def norm_mixed(m):
                act.wait_ge(rs_m_done, m)
                for j in range(TT):
                    nc.scalar.activation(xr[:, j, :], x1[:, j, :], ACT.Copy,
                                         scale=rs_m[:, j:j + 1]).then_inc(x1n_done, 1)

            def split_h2(m, d):
                act.wait_ge(transposed, DT * m + d + 1)
                nc.scalar.activation(h2_hi[:, d, :], h2_bank(m, d), ACT.Copy,
                                     scale=g_mlp_c[:, d:d + 1]).then_inc(h2_hi_done, 1)

            def final_stats(g, outs_before):
                for j in range(TT if g is not LAST else TT - 1):
                    act.wait_ge(ring_read, outs_before + NH * (j + 1))
                    if j > 0:
                        act.wait_ge(ms_f_done, TT * g + j)
                    mean_square(acc[:, j, :], ms_f[:, j:j + 1]).then_inc(ms_f_done, 1)
                if g is LAST:
                    j = TT - 1
                    for h, dst in ((0, ms_f[:, j:j + 1]), (1, ms_end[:, :])):
                        act.wait_ge(ring_read, outs_before + NH * j + h + 1)
                        act.wait_ge(ms_f_done, TT * g + j + h)
                        mean_square(acc[:, j, h * HALF:(h + 1) * HALF], dst,
                                    squares=junk[:, h * HALF:(h + 1) * HALF]).then_inc(ms_f_done, 1)

            act.wait_ge(const_set, 3)
            mean_square(eps[:, 0:1], warm[:, :], squares=warm_square)
            for i in ACT_TILES:
                act.wait_ge(first_in[i], 16)
                n = ROW_N[i]
                mean_square(first_x[0:n, i, :], ms_x[0:n, i:i + 1], n, row_squares[i]).then_inc(first_ms_done[i], 1)

            def first_split(w):
                for c in range(CT):
                    act.wait_ge(banded, CT * w + c + 1)
                    nc.scalar.copy(first_dt[w][0][:, c, :], first_banks[w][:, c, :]).then_inc(first_hi_done, 1)

            def first_mixed_stats(i):
                for j in range(TT):
                    n = TT * i + j
                    slot, c = n % SLOTS, slice(i * WC, (i + 1) * WC)
                    act.wait_ge(ring_read, n + 1)
                    if n >= SLOTS:
                        act.wait_ge(ms_part_done, n + 1 - SLOTS)
                    mean_square(x1[:, j, c], ms_part[:, i, j:j + 1],
                                squares=first_squares[:, slot * WC:(slot + 1) * WC]).then_inc(ms_part_done, 1)

            def split_pool_w(w):
                act.wait_ge(pool_scaled, CT * (w + 1))
                part = slice(w * CT, (w + 1) * CT)
                nc.scalar.copy(pw_hi[:, part, :], pw_raw[:, part, :]).then_inc(pool_hi, 1)

            act.wait_ge(band_in[1], 16)
            for i in (4, 2):
                act.wait_ge(first_rs_done, TILE_ORDER.index(i) + 1)
                n = ROW_N[i]
                nc.scalar.activation(band_x[0:n, i, :, 0:OUT_N[i]], band[0:n, 1, :, 0:OUT_N[i]], ACT.Copy,
                                     scale=rs_x[0:n, i:i + 1]).then_inc(band_scaled[i], 1)
            split_pool_w(0)
            first_split(0)
            first_split(1)
            split_pool_w(1)
            first_split(2)
            first_split(3)
            split_pool_w(2)
            split_pool_w(3)
            first_mixed_stats(0)
            split_wu(0, 0, first=True)
            for i in range(1, WINDOWS):
                first_mixed_stats(i)
            for j, h in ((0, 0), (3, 0), (0, 1)):
                c = slice(h * HALF, (h + 1) * HALF)
                act.wait_ge(first_rs_m_done, j // 2 + 1)
                nc.scalar.activation(xr[:, j, c], x1[:, j, c], ACT.Copy,
                                     scale=rs_m[:, j:j + 1]).then_inc(first_x1n[h], 1)
            act.wait_ge(gain_in, 32)
            for d in range(DT):
                split_h2(FIRST, d)
                if d == DT // 2:
                    split_wu(0, 1, first=True)
            follow_up(0, 0, first=True)

            def pair(n, outs):
                split_wd(n - 1, outs)
                follow_up(n, 1)
                split_wd(n, outs + OUTS)
                follow_up(n + 1, 0)

            def mix_pair(g, w):
                n = CHUNKS * g + 2 * w + 1
                outs = ring_base(g) + w * MIX_PAIR_OUTS
                split_wd(n - 1, outs)
                if w == 0:
                    row_stats(g + 1)
                follow_up(n, 1)
                norm_rows(g + 1, w)
                if w > 0:
                    act.wait_ge(dt_lo_done, WINDOWS * g + w)
                keep_turned(g + 1, w)
                split_wd(n, outs + OUTS)
                follow_up(n + 1, 0)
                split_pooled(g + 1, w)

            with act.Fori(0, GROUPS - 1) as g:
                n0 = CHUNKS * g
                outs = ring_base(g)
                for w in range(MIX_PAIRS):
                    mix_pair(g, w)
                n = n0 + 2 * MIX_PAIRS + 1
                split_wd(n - 1, outs + MIX_END)
                follow_up(n, 1)
                mixed_stats(g + 1, outs + MIX_END)
                norm_mixed(g + 1)
                split_wd(n, outs + MIX_END + OUTS)
                follow_up(n + 1, 0)
                with act.Fori(1, PAIRS - 1 - MIX_PAIRS) as i:
                    pair(n0 + 2 * (i + MIX_PAIRS) + 1, outs + MIX_END + i * PAIR_OUTS)
                last = outs + GROUP_OUTS - PAIR_OUTS
                n = n0 + CHUNKS - 1
                split_wd(n - 1, last)
                activate(n, 1, 0)
                split_wu(n + 1, 0)
                activate(n, 1, 1)
                split_h2(g + 1, 0)
                split_h2(g + 1, 1)
                split_wu(n + 1, 1)
                for d in range(2, DT):
                    split_h2(g + 1, d)
                split_wd(n, last + OUTS)
                follow_up(n + 1, 0)
                final_stats(g, last + OUTS)
                act.wait_ge(ms_f_done, TT * (g + 1))
            n0 = CHUNKS * (GROUPS - 1)
            with act.Fori(0, PAIRS - 1) as i:
                pair(n0 + 2 * i + 1, LAST_BASE + i * PAIR_OUTS)
            last = LAST_BASE + (PAIRS - 1) * PAIR_OUTS
            split_wd(n0 + CHUNKS - 2, last)
            n = n0 + CHUNKS - 1
            for t in range(FT):
                activate(n, 1, t)
            for t in range(FT):
                act.wait_ge(wd_in, 16 * (n + 1))
                act.wait_ge(up_done, FT * (n + 1))
                nc.scalar.copy(wd_last_hi[:, NH * t:NH * (t + 1), :],
                               wd_raw[:, t, :].rearrange("p (h e) -> p h e", h=NH)).then_inc(wd_hi_done, 1)
            final_stats(LAST, last + OUTS)

        @block.vector
        def _(dve):
            def split_wu(n, t):
                dve.wait_ge(wu_hi_done, FT * n + t + 1)
                nc.vector.tensor_tensor(wu_lo[:, t, :, :], wu_raw[:, t, :, :], wu_hi[:, t, :, :].bitcast(f32),
                                        ALU.subtract).then_inc(wu_lo_done, 1)

            def split_wd(n):
                for t in range(FT):
                    dve.wait_ge(wd_hi_done, FT * n + t + 1)
                    nc.vector.tensor_tensor(wd_lo[:, t, :], wd_raw[:, t, :], wd_hi[:, t, :].bitcast(f32),
                                            ALU.subtract).then_inc(wd_lo_done, 1)

            def split_a(n, slot, t):
                dve.wait_ge(a_hi_done, FT * n + t + 1)
                dve.wait_ge(square_done, FT * n + t + 1)
                nc.vector.tensor_tensor(a_lo[:, slot, t, :], square[:, t, :], a_hi[:, slot, t, :].bitcast(f32),
                                        ALU.subtract).then_inc(a_lo_done, 1)

            def add_down(outs, o, base=acc):
                j, c = o // NH, slice((o % NH) * HALF, (o % NH + 1) * HALF)
                dve.wait_ge(ring_full, outs + o + 1)
                nc.vector.tensor_tensor(acc[:, j, c], ring_ps[:, o % RING, :], base[:, j, c],
                                        ALU.add).then_inc(ring_read, 1)

            def add_pooled(m, w, outs, bank=lambda w, j: ring_ps[:, j, :]):
                for j in range(TT):
                    c = ds(w * WC, WC)
                    dve.wait_ge(ring_full, outs + j + 1)
                    nc.vector.tensor_tensor(x1[:, j, c], bank(w, j)[:, 0:WC], xr[:, j, c],
                                            ALU.add).then_inc(ring_read, 1)

            def subtract_own(m, w):
                dve.wait_ge(summed, SUM_STEPS[WINDOWS] * (m - 1) + SUM_STEPS[w + 1])
                s = sums[w % 2][:, :, HALO:HALO + GT]
                nc.vector.scalar_tensor_tensor(s, s, 0.5 ** (w + 1), ht[:, :, HALO:HALO + GT],
                                               ALU.mult, ALU.subtract).then_inc(diff_done, 1)

            def split_pooled(m, w):
                dve.wait_ge(dt_hi_done, WINDOWS * (m - 1) + w + 1)
                nc.vector.tensor_tensor(dt_lo[:, :, :], sums[w % 2][:, :, HALO:HALO + GT],
                                        dt_hi[:, :, :].bitcast(f32), ALU.subtract).then_inc(dt_lo_done, 1)

            def split_h2(m, d):
                dve.wait_ge(h2_hi_done, DT * m + d + 1)
                nc.vector.scalar_tensor_tensor(h2_lo[:, d, :], h2_bank(m, d), g_mlp_c[:, d:d + 1],
                                               h2_hi[:, d, :].bitcast(f32),
                                               ALU.mult, ALU.subtract).then_inc(h2_lo_done, 1)

            def finish(g, j):
                dve.wait_ge(rs_f_done, TT * g + j + 1)
                nc.vector.scalar_tensor_tensor(acc[:, j, :], acc[:, j, :], rs_f[:, j:j + 1], g_fin_b[:, :],
                                               ALU.mult, ALU.mult).then_inc(final_done, 1)

            nc.vector.memset(power[:, :], -0.5).then_inc(const_set, 1)
            nc.vector.memset(eps[:, :], EPS).then_inc(const_set, 1)
            nc.vector.memset(ms_x[:, :], 1.0).then_inc(const_set, 1)
            dve.wait_ge(const_set, 3)

            def scale_band(i):
                dve.wait_ge(band_in[min(i, 1)], 16)
                dve.wait_ge(first_rs_done, TILE_ORDER.index(i) + 1)
                nc.vector.tensor_scalar(band_x[:, i, :, 0:OUT_N[i]], band[:, min(i, 1), :, 0:OUT_N[i]],
                                        rs_x[:, i:i + 1], None, ALU.mult).then_inc(band_scaled[i], 1)

            scale_band(0)
            scale_band(1)
            for i in DVE_TILES:
                dve.wait_ge(first_in[i], 16)
                nc.vector.scalar_tensor_tensor(row_squares[i], first_x[:, i, :], 1.0 / D, first_x[:, i, :],
                                               ALU.mult, ALU.mult,
                                               accum_out=ms_x[:, i:i + 1]).then_inc(first_ms_done[i], 1)
            nc.vector.memset(xw[:, TT, :], 0.0).then_inc(const_set, 1)
            scale_band(3)

            def scale_pool_w(w):
                dve.wait_ge(pw_in[w], 16)
                for q in range(w * CT, (w + 1) * CT):
                    nc.vector.scalar_tensor_tensor(pw_raw[:, q, :], pw_raw[:, q, :], g_mix_c[:, q:q + 1],
                                                   scale_b[:, (q // CT) * WC:(q // CT + 1) * WC],
                                                   ALU.mult, ALU.mult).then_inc(pool_scaled, 1)

            def first_split(w):
                hi, lo = first_dt[w]
                for c in range(CT):
                    dve.wait_ge(first_hi_done, CT * w + c + 1)
                    nc.vector.tensor_tensor(lo[:, c, :], first_banks[w][:, c, :], hi[:, c, :].bitcast(f32),
                                            ALU.subtract).then_inc(first_lo_done, 1)

            dve.wait_ge(acc_moved, ACC_LOADS)
            dve.wait_ge(g_mix_in, 16)
            for w in range(WINDOWS - 1):
                scale_pool_w(w)
            first_split(0)
            first_split(1)
            scale_pool_w(WINDOWS - 1)
            first_split(2)
            first_split(3)
            for j in range(TT):
                dve.wait_ge(xr_in[j], 16)
            for w in range(WINDOWS):
                add_pooled(0, w, w * TT, bank=first_out_bank)
            for j, h in ((1, 0), (1, 1), (2, 0), (2, 1), (3, 1)):
                c = slice(h * HALF, (h + 1) * HALF)
                dve.wait_ge(first_rs_m_done, j // 2 + 1)
                nc.vector.tensor_scalar(xr[:, j, c], x1[:, j, c], rs_m[:, j:j + 1], None,
                                        ALU.mult).then_inc(first_x1n[h], 1)
            dve.wait_ge(gain_in, 32)
            for d in range(DT):
                split_h2(FIRST, d)
            dve.wait_ge(wu_lo_done, FT)
            split_wu(1, 0)
            split_wu(1, 1)

            def step(n, slot, outs, after={}, first_of=None):
                split_wd(n - 1)
                for t in range(FT):
                    split_a(n - 1, slot, t)
                split_wu(n + 1, 0)
                if first_of is not None:
                    dve.wait_ge(acc_moved, ACC_LOADS + 16 * TT * first_of)
                for o in range(OUTS):
                    add_down(outs, o, acc if first_of is None else x1)
                    if o == 0:
                        split_wu(n + 1, 1)
                    for work in after.get(o, []):
                        work()

            def pair(n, outs, first_of=None):
                step(n, 0, outs, first_of=first_of)
                step(n + 1, 1, outs + OUTS)

            def mix_pair(g, w):
                n = CHUNKS * g + 2 * w + 1
                outs = ring_base(g) + w * MIX_PAIR_OUTS
                step(n, 0, outs, first_of=g if w == 0 else None)
                step(n + 1, 1, outs + OUTS, {2: [lambda: subtract_own(g + 1, w)],
                                             4: [lambda: split_pooled(g + 1, w)]})
                add_pooled(g + 1, w, outs + PAIR_OUTS)

            with dve.Fori(0, GROUPS - 1) as g:
                n0 = CHUNKS * g
                outs = ring_base(g)
                for w in range(MIX_PAIRS):
                    mix_pair(g, w)
                with dve.Fori(MIX_PAIRS, PAIRS - 1) as i:
                    pair(n0 + 2 * i + 1, outs + WINDOWS * TT + i * PAIR_OUTS)
                n = n0 + CHUNKS - 1
                last = outs + GROUP_OUTS - PAIR_OUTS
                split_wd(n - 1)
                split_a(n - 1, 0, 0)
                split_a(n - 1, 0, 1)
                split_wu(n + 1, 0)
                split_h2(g + 1, 0)
                split_h2(g + 1, 1)
                for o in range(OUTS):
                    add_down(last, o)
                    if o == 0:
                        split_wu(n + 1, 1)
                    elif o + 1 < DT:
                        split_h2(g + 1, o + 1)
                step(n + 1, 1, last + OUTS,
                     {NH * (j + 2) - 1: [lambda j=j: finish(g, j)] for j in range(TT - 1)})
                finish(g, TT - 1)
            g = LAST
            n0 = CHUNKS * g
            pair(n0 + 1, LAST_BASE, first_of=g)
            with dve.Fori(1, PAIRS - 1) as i:
                pair(n0 + 2 * i + 1, LAST_BASE + i * PAIR_OUTS)
            n = n0 + CHUNKS - 1
            last = LAST_BASE + (PAIRS - 1) * PAIR_OUTS
            split_wd(n - 1)
            split_a(n - 1, 0, 0)
            split_a(n - 1, 0, 1)
            for o in range(OUTS):
                add_down(last, o)
                if 2 <= o < 2 + FT:
                    t = o - 2
                    split_a(n, 1, t)
                    dve.wait_ge(wd_hi_done, FT * n + t + 1)
                    nc.vector.tensor_tensor(wd_last_lo[:, NH * t:NH * (t + 1), :],
                                            wd_raw[:, t, :].rearrange("p (h e) -> p h e", h=NH),
                                            wd_last_hi[:, NH * t:NH * (t + 1), :].bitcast(f32),
                                            ALU.subtract).then_inc(wd_lo_done, 1)
            for o in range(OUTS):
                add_down(last + OUTS, o)
                if o % NH == NH - 1 and o >= 2 * NH - 1:
                    finish(g, o // NH - 1)
            for h in range(NH):
                c = slice(h * HALF, (h + 1) * HALF)
                dve.wait_ge(rs_f_done, TT * GROUPS)
                nc.vector.scalar_tensor_tensor(acc[:, TT - 1, c], acc[:, TT - 1, c], rs_f[:, TT - 1:TT],
                                               g_fin_b[:, c], ALU.mult, ALU.mult).then_inc(final_done, 1)

        @block.gpsimd
        def _(pool):
            def squares(n, first=False):
                for t in range(FT):
                    pool.wait_ge(relu_done, FT * n + t + 1)
                    if not first:
                        pool.wait_ge(a_lo_done, FT * (n - 1) + t + 1)
                    nc.gpsimd.tensor_tensor(square[:, t, :], relu[:, t, :], relu[:, t, :],
                                            ALU.mult).then_inc(square_done, 1)

            def rms(ms, me, rs, width, me_sem, count, rs_sem, add=None):
                nc.gpsimd.tensor_tensor(me, ms, eps[:, 0:width] if add is None else add, ALU.add).then_inc(me_sem, 1)
                pool.wait_ge(me_sem, count)
                nc.gpsimd.tensor_tensor(rs, me, power[:, 0:width], ALU.pow).then_inc(rs_sem, 1)

            def row_rms(m):
                pool.wait_ge(ms_x_done, NORMS * m)
                rms(ms_x[:, :], me_x[:, :], rs_x[:, :], NORMS, me_x_done, m, rs_x_done)

            def mixed_rms(m):
                pool.wait_ge(ms_m_done, TT * m)
                rms(ms_m[:, :], me_m[:, :], rs_m[:, :], TT, me_m_done, WINDOWS + 1 + m, rs_m_done)

            def final_rms(g):
                for j in range(TT if g is not LAST else TT - 1):
                    c = slice(j, j + 1)
                    pool.wait_ge(ms_f_done, TT * g + j + 1)
                    rms(ms_f[:, c], me_f[:, c], rs_f[:, c], 1, me_f_done, TT * g + j + 1, rs_f_done)

            def next_sums(m, w):
                pool.wait_ge(ends_in, 16 * m)
                pool.wait_ge(ht_done, TURNS * (WINDOWS * (m - 1) + w + 1))
                window_sums(nc.gpsimd, pool, w, ht, sums, summed,
                            SUM_STEPS[WINDOWS] * (m - 1) + SUM_STEPS[w])

            pool.wait_ge(const_set, 3)
            for k, i in enumerate(TILE_ORDER):
                c = slice(i, i + 1)
                pool.wait_ge(first_ms_done[i], 1)
                rms(ms_x[:, c], me_x[:, c], rs_x[:, c], 1, first_me_done, k + 1, first_rs_done)
            for w in range(WINDOWS):
                part = slice(w * CT, (w + 1) * CT)
                pool.wait_ge(pool_hi, w + 1)
                nc.gpsimd.tensor_tensor(pw_lo[:, part, :], pw_raw[:, part, :], pw_hi[:, part, :].bitcast(f32),
                                        ALU.subtract).then_inc(pool_lo, 1)
            def split_first_wu(t):
                pool.wait_ge(wu_hi_done, t + 1)
                nc.gpsimd.tensor_tensor(wu_lo[:, t, :, :], wu_raw[:, t, :, :], wu_hi[:, t, :, :].bitcast(f32),
                                        ALU.subtract).then_inc(wu_lo_done, 1)

            split_first_wu(0)
            for i in range(WINDOWS - 1):
                pool.wait_ge(ms_part_done, TT * (i + 1))
                if i > 0:
                    pool.wait_ge(me_m_done, i)
                nc.gpsimd.tensor_tensor(me_m[:, :], ms_part[:, i, :], me_m[:, :] if i > 0 else eps[:, 0:TT],
                                        ALU.add).then_inc(me_m_done, 1)
            pool.wait_ge(me_m_done, WINDOWS - 1)
            for h in range(2):
                c = slice(h * TT // 2, (h + 1) * TT // 2)
                pool.wait_ge(ms_part_done, TT * (WINDOWS - 1) + (h + 1) * TT // 2)
                rms(ms_part[:, WINDOWS - 1, c], me_m[:, c], rs_m[:, c], TT // 2, me_m_done, WINDOWS + h,
                    first_rs_m_done, me_m[:, c])
            split_first_wu(1)
            squares(0, first=True)
            with pool.Fori(0, GROUPS - 1) as g:
                n0 = CHUNKS * g
                row_rms(g + 1)
                for w in range(MIX_PAIRS):
                    squares(n0 + 2 * w + 1)
                    next_sums(g + 1, w)
                    squares(n0 + 2 * w + 2)
                squares(n0 + 2 * MIX_PAIRS + 1)
                mixed_rms(g + 1)
                with pool.Fori(2 * MIX_PAIRS + 1, CHUNKS) as i:
                    squares(n0 + i + 1)
                final_rms(g)
            n0 = CHUNKS * (GROUPS - 1)
            with pool.Fori(1, CHUNKS) as i:
                squares(n0 + i)
            final_rms(LAST)
            c = slice(TT - 1, TT)
            pool.wait_ge(ms_f_done, TT * GROUPS)
            nc.gpsimd.tensor_tensor(me_end[:, :], ms_f[:, c], eps[:, 0:1], ALU.add).then_inc(me_f_done, 1)
            pool.wait_ge(me_f_done, TT * GROUPS)
            pool.wait_ge(ms_f_done, TT * GROUPS + 1)
            rms(me_end[:, :], me_f[:, c], rs_f[:, c], 1, me_f_done, TT * GROUPS + 1, rs_f_done, ms_end[:, :])

        @block.tensor
        def _(pe):
            def up_tile(n, t, each=lambda d: None):
                pe.wait_ge(wu_lo_done, FT * n + t + 1)
                for d in range(DT):
                    each(d)
                    o = up_ps[:, t, :]
                    nc.tensor.matmul(o, wu_hi[:, t, d, :], h2_hi[:, d, :], start=(d == 0), stop=False)
                    nc.tensor.matmul(o, wu_hi[:, t, d, :], h2_lo[:, d, :], start=False, stop=False)
                    last = nc.tensor.matmul(o, wu_lo[:, t, d, :], h2_hi[:, d, :], start=False, stop=(d == DT - 1))
                last.then_inc(up_done, 1)

            def up(n, each=lambda d: None):
                for t in range(FT):
                    pe.wait_ge(relu_done, FT * (n - 1) + t + 1)
                    up_tile(n, t, each if t == 0 else lambda d: None)

            def down_out(slot, outs, o, final=False):
                j, h = o // NH, o % NH
                r = slice(j * P, (j + 1) * P)
                c = slice(h * HALF, (h + 1) * HALF)
                pe.wait_ge(ring_read, outs + o + 1 - RING)
                dst = ring_ps[:, o % RING, :]
                for t in range(FT):
                    hi, lo = wd_hi[:, t, c], wd_lo[:, t, c]
                    if final:
                        hi, lo = wd_last_hi[:, NH * t + h, :], wd_last_lo[:, NH * t + h, :]
                    nc.tensor.matmul(dst, a_hi[:, slot, t, r], hi, start=(t == 0), stop=False)
                    nc.tensor.matmul(dst, a_hi[:, slot, t, r], lo, start=False, stop=False)
                    last = nc.tensor.matmul(dst, a_lo[:, slot, t, r], hi, start=False, stop=(t == FT - 1))
                last.then_inc(ring_full, 1)

            def down_ready(n):
                pe.wait_ge(wd_lo_done, FT * (n + 1))
                pe.wait_ge(a_lo_done, FT * (n + 1))

            def down(n, slot, outs, final=False, after={}):
                down_ready(n)
                for o in range(OUTS):
                    down_out(slot, outs, o, final)
                    for work in after.get(o, []):
                        work()

            def turn_window(m, w):
                v = WINDOWS * (m - 1) + w
                pe.wait_ge(xw_done, NORMS * (v + 1))
                for c in range(CT):
                    for j in range(TT):
                        last = nc.tensor.transpose(mix_ps[:, c, j * P:(j + 1) * P],
                                                   xw[:, j, c * P:(c + 1) * P], ident[:, :])
                    last.then_inc(x_turned, 1)

            def turn_halos(m, w):
                pe.wait_ge(ht_done, TURNS * (WINDOWS * (m - 1) + w) + 1)
                for c in range(CT):
                    last = nc.tensor.transpose(mix_ps[:, 0, c * P:(c + 1) * P],
                                               xw[:, TT, c * P:(c + 1) * P], ident[:, :])
                last.then_inc(x_turned, 1)

            def pool_tile(w, j, dst, hi=dt_hi, lo=dt_lo):
                r = slice(j * P, (j + 1) * P)
                for c in range(CT):
                    q = w * CT + c
                    nc.tensor.matmul(dst, hi[:, c, r], pw_hi[:, q, :], start=(c == 0), stop=False)
                    nc.tensor.matmul(dst, hi[:, c, r], pw_lo[:, q, :], start=False, stop=False)
                    last = nc.tensor.matmul(dst, lo[:, c, r], pw_hi[:, q, :], start=False, stop=(c == CT - 1))
                last.then_inc(ring_full, 1)

            def pool_out(m, w, outs):
                pe.wait_ge(dt_lo_done, WINDOWS * (m - 1) + w + 1)
                for j in range(TT):
                    pe.wait_ge(ring_read, outs + j + 1 - RING)
                    pool_tile(w, j, ring_ps[:, j, 0:WC])

            def transpose(m, d):
                if m is FIRST:
                    if d >= 6:
                        pe.wait_ge(h2_lo_done, d - 5)
                elif d < 2:
                    pe.wait_ge(ht_done, TURNS * WINDOWS * m)
                else:
                    pe.wait_ge(h2_lo_done, DT * m + d - 1)
                for j in range(TT):
                    last = nc.tensor.transpose(h2_bank(m, d)[:, j * P:(j + 1) * P],
                                               xr[:, j, d * P:(d + 1) * P], ident[:, :])
                last.then_inc(transposed, 1)

            pe.wait_ge(ident_loaded, 16)
            def keep_clock(count):
                for _ in range(count):
                    nc.tensor.transpose(ring_ps[:, 3, 0:P], ident[:, :], ident[:, :])

            keep_clock(WARM_UP[0])
            for i in TILE_ORDER:
                n = ROW_N[i]
                pe.wait_ge(band_scaled[i], 1)
                for w in range(WINDOWS):
                    for c in range(CT):
                        ch = slice(w * WC + c * P, w * WC + (c + 1) * P)
                        last = nc.tensor.matmul(first_banks[w][:, c, OUT_AT[i]:OUT_AT[i] + OUT_N[i]],
                                                first_x[0:n, i, ch], band_x[0:n, i, w, 0:OUT_N[i]],
                                                start=True, stop=True)
                        if i == TILE_ORDER[-1]:
                            last.then_inc(banded, 1)

            for w in range(WINDOWS):
                pe.wait_ge(pool_lo, w + 1)
                for j in range(TT):
                    if w < 2:
                        pe.wait_ge(first_lo_done, max(CT * (w + 1), TT * w + j + 1))
                    else:
                        pe.wait_ge(ring_read, TT * (w - 1) + j + 1)
                    pool_tile(w, j, first_out_bank(w, j)[:, 0:WC], *first_dt[w])

            pe.wait_ge(ring_read, FIRST_OUTS)
            keep_clock(WARM_UP[1])

            def first_transpose(d):
                pe.wait_ge(first_x1n[d // (DT // NH)], TT)
                transpose(FIRST, d)

            for d in range(DT // NH):
                first_transpose(d)

            def next_tile(d):
                if d + DT // NH < DT:
                    first_transpose(d + DT // NH)
                pe.wait_ge(h2_lo_done, d + 1)

            up_tile(0, 0, next_tile)
            up_tile(0, 1)

            with pe.Fori(0, GROUPS - 1) as g:
                n0 = CHUNKS * g
                outs = ring_base(g)
                with pe.Fori(0, MIX_PAIRS) as w:
                    n = n0 + 2 * w + 1
                    outs_w = outs + w * MIX_PAIR_OUTS
                    up(n)
                    pe.wait_ge(h2_lo_done, DT * (g + 1))
                    down(n - 1, 0, outs_w, after={5: [lambda: turn_window(g + 1, w)],
                                                  7: [lambda: turn_halos(g + 1, w)]})
                    up(n + 1)
                    down(n, 1, outs_w + OUTS)
                    pool_out(g + 1, w, outs_w + PAIR_OUTS)
                with pe.Fori(0, PAIRS - 1 - MIX_PAIRS) as i:
                    n = n0 + 2 * (i + MIX_PAIRS) + 1
                    outs_i = outs + MIX_END + i * PAIR_OUTS
                    up(n)
                    down(n - 1, 0, outs_i)
                    up(n + 1)
                    down(n, 1, outs_i + OUTS)
                n = n0 + CHUNKS - 1
                last = outs + GROUP_OUTS - PAIR_OUTS
                up(n)
                down_ready(n - 1)
                pe.wait_ge(x1n_done, TT * (g + 1))
                transpose(g + 1, 0)
                transpose(g + 1, 1)
                for o in range(OUTS):
                    down_out(0, last, o)
                    if 0 < o < DT - 1:
                        transpose(g + 1, o + 1)
                pe.wait_ge(h2_lo_done, DT * (g + 2) - 1)

                def last_tile(d):
                    if d == DT - 1:
                        pe.wait_ge(h2_lo_done, DT * (g + 2))

                up(n + 1, last_tile)
                down(n, 1, last + OUTS)
            n0 = CHUNKS * (GROUPS - 1)
            with pe.Fori(0, PAIRS - 1) as i:
                n = n0 + 2 * i + 1
                outs_i = LAST_BASE + i * PAIR_OUTS
                up(n)
                down(n - 1, 0, outs_i)
                up(n + 1)
                down(n, 1, outs_i + OUTS)
            n = n0 + CHUNKS - 1
            last = LAST_BASE + (PAIRS - 1) * PAIR_OUTS
            up(n)
            down(n - 1, 0, last)
            down(n, 1, last + OUTS, final=True)


def end_scales():
    import numpy as np

    scale = np.ones((GROUPS, WINDOWS, 2, HALO), np.float32)
    for w in range(WINDOWS):
        half = 2 ** w
        for t in range(HALO):
            for g in (0, GROUPS - 1):
                scale[g, w, 0, t] = 2 * half / (min(t, half) + half)
            for g in (GROUPS - 2, GROUPS - 1):
                scale[g, w, 1, t] = 2 * half / (half + min(HALO - t, half))
    scale = np.broadcast_to(scale[:, None, :, None], (GROUPS, P, WINDOWS, CT, 2, HALO))
    return np.ascontiguousarray(scale)


def pool_bands():
    import numpy as np

    bands = np.zeros((P, 2, WINDOWS, BAND), np.float32)
    for w in range(WINDOWS):
        half = 2 ** w
        for tile in range(2):
            for c in range(OUT_N[tile]):
                t = OUT_AT[tile] - ROW_AT[tile] + c
                before = min(t, half)
                bands[t - before:t + half, tile, w, c] = 1 / (before + half)
                bands[t, tile, w, c] -= 1
    return bands


def kernel(x_prompt, x_sample, norm_mix_g, norm_mlp_g, w_up, w_down, final_norm_g, pool_w, pool_scale, **unused):
    import concourse.bacc as bacc
    import numpy as np
    from concourse.bass_utils import run_bass_kernel_spmd

    seqs = [np.asarray(x_prompt)[0], np.asarray(x_sample)[0]]
    halos = []
    for seq in seqs:
        edge = np.zeros((HALO, D), np.float32)
        rows = np.concatenate([edge, seq, edge])
        for at in range(0, len(seq), GT):
            halos.append(np.concatenate([rows[at:at + HALO], rows[at + HALO + GT:at + HT]]))
    arrays = {
        "x": np.concatenate(seqs).reshape(GROUPS, GT, D),
        "halos": np.stack(halos),
        "w_up": np.ascontiguousarray(np.asarray(w_up)[0].reshape(DT, P, CHUNKS, FT, P).transpose(2, 3, 1, 0, 4)),
        "w_down": np.ascontiguousarray(np.asarray(w_down)[0].reshape(CHUNKS, FT, P, D).transpose(0, 2, 1, 3)),
        "pool_w": np.ascontiguousarray(np.asarray(pool_w)[0]),
        "pool_scale": np.ascontiguousarray(np.asarray(pool_scale)[0]),
        "g_mix": np.ascontiguousarray(np.asarray(norm_mix_g)[0].reshape(DT, P).T),
        "g_mlp": np.ascontiguousarray(np.asarray(norm_mlp_g)[0].reshape(DT, P).T),
        "g_fin": np.ascontiguousarray(np.asarray(final_norm_g)),
        "ends": end_scales(),
        "bands": pool_bands(),
        "ident_in": np.eye(P, dtype=np.float32),
    }
    nc = bacc.Bacc("TRN2", target_bir_lowering=False, num_devices=1)
    args = [nc.dram_tensor(name, a.shape, mybir.dt.float32, kind="ExternalInput").ap() for name, a in arrays.items()]
    out = nc.dram_tensor("out", (GROUPS, GT, D), mybir.dt.float32, kind="ExternalOutput").ap()
    build(nc, *args, out)
    r = run_bass_kernel_spmd(nc, [arrays], core_ids=[0])
    y = r.results[0]["out"].reshape(1, GROUPS * GT, D)
    n = len(seqs[0])
    return y[:, :n], y[:, n:]
```
